# Optimizing a Trainium2 kernel written in Bass

```python
import math
import jax, jax.numpy as jnp
from jax import lax
import numpy as np

D_MODEL = 1024
BATCH = 1
SEQ = 512
DEPTH = 2

CHUNK = 64
Q_BLOCK = 128
NH_A = 4
HD_A = 64
NH_B = 8
NOPE_B = 64
ROPE_B = 32
V_B = 64
Q_LORA = 256
KV_LORA = 128
ROPE_THETA = 10000.0
NH_C = 4
NKV_C = 2
HD_C = 64
WINDOW = 128
WINDOW_CHUNKS = WINDOW // CHUNK
MIX = NH_A * HD_A + NH_B * V_B + NH_C * HD_C
SPLIT_SIZES = (NH_A * HD_A, NH_A * HD_A, NH_A * HD_A,
               Q_LORA, KV_LORA, ROPE_B,
               NH_C * HD_C, NKV_C * HD_C, NKV_C * HD_C)
IN_COLS = sum(SPLIT_SIZES)
D_FF = 4 * D_MODEL
ALPHA = (2 * DEPTH) ** 0.25
BETA = (8 * DEPTH) ** -0.25
LN_EPS = 1e-5
NEG_INF = -1e30

kernel_name = 'hybrid_sb_mla_swa_deepnorm_adaln'

def layer_norm(x, g, b):
    xf = x.astype(jnp.float32)
    mu = jnp.mean(xf, axis=-1, keepdims=True)
    var = jnp.mean(jnp.square(xf - mu), axis=-1, keepdims=True)
    return ((xf - mu) * lax.rsqrt(var + LN_EPS) * g + b).astype(x.dtype)

def rms_norm(x, g):
    xf = x.astype(jnp.float32)
    y = xf * lax.rsqrt(jnp.mean(jnp.square(xf), axis=-1, keepdims=True) + LN_EPS)
    return (y * g).astype(x.dtype)

def rope(x, positions):
    d = x.shape[-1]
    inv_freq = 1.0 / (ROPE_THETA ** (jnp.arange(0, d, 2, dtype=jnp.float32) / d))
    ang = positions.astype(jnp.float32)[..., None] * inv_freq
    cos, sin = jnp.cos(ang)[:, :, None, :], jnp.sin(ang)[:, :, None, :]
    xf = x.astype(jnp.float32)
    x1, x2 = xf[..., : d // 2], xf[..., d // 2:]
    return jnp.concatenate([x1 * cos - x2 * sin, x1 * sin + x2 * cos], axis=-1).astype(x.dtype)

def to_query_blocks(q):
    B, S, H, d = q.shape
    return q.reshape(B, S // Q_BLOCK, Q_BLOCK, H, d).transpose(1, 0, 2, 3, 4)

def from_query_blocks(o):
    nb, B, QB, H, d = o.shape
    return o.transpose(1, 0, 2, 3, 4).reshape(B, nb * QB, H, d)

def stick_breaking_attention(q, k, v):
    dtype = q.dtype
    S, d = q.shape[1], q.shape[-1]
    qf, kf, vf = q.astype(jnp.float32), k.astype(jnp.float32), v.astype(jnp.float32)
    key_idx = jnp.arange(S, dtype=jnp.int32)
    starts = jnp.arange(S // Q_BLOCK, dtype=jnp.int32) * Q_BLOCK
    scale = 1.0 / math.sqrt(d)

    def block(args):
        q_blk, start = args
        z = jnp.einsum('bqhd,bkhd->bhqk', q_blk, kf) * scale
        q_idx = start + jnp.arange(Q_BLOCK, dtype=jnp.int32)
        causal = key_idx[None, :] < q_idx[:, None]
        log_1m = jnp.where(causal, jax.nn.log_sigmoid(-z), 0.0)
        suffix = lax.cumsum(log_1m, axis=3, reverse=True) - log_1m
        w = jnp.where(causal, jnp.exp(jax.nn.log_sigmoid(z) + suffix), 0.0)
        return jnp.einsum('bhqk,bkhd->bqhd', w, vf)

    out = lax.map(block, (to_query_blocks(qf), starts))
    return from_query_blocks(out).astype(dtype)

def chunk_causal_attention(q, k, v):
    dtype = q.dtype
    S, d = q.shape[1], q.shape[-1]
    qf, kf, vf = q.astype(jnp.float32), k.astype(jnp.float32), v.astype(jnp.float32)
    key_chunk = jnp.arange(S, dtype=jnp.int32) // CHUNK
    starts = jnp.arange(S // Q_BLOCK, dtype=jnp.int32) * Q_BLOCK
    scale = 1.0 / math.sqrt(d)

    def block(args):
        q_blk, start = args
        s = jnp.einsum('bqhd,bkhd->bhqk', q_blk, kf) * scale
        q_chunk = (start + jnp.arange(Q_BLOCK, dtype=jnp.int32)) // CHUNK
        allowed = key_chunk[None, :] <= q_chunk[:, None]
        p = jax.nn.softmax(jnp.where(allowed, s, NEG_INF), axis=-1)
        return jnp.einsum('bhqk,bkhd->bqhd', p, vf)

    out = lax.map(block, (to_query_blocks(qf), starts))
    return from_query_blocks(out).astype(dtype)

def sliding_window_gqa(q, k, v, positions, sinks):
    dtype = q.dtype
    B, S, Hq, d = q.shape
    Hkv = k.shape[2]
    G = Hq // Hkv
    W = WINDOW_CHUNKS
    nC = S // CHUNK
    qf, kf, vf = q.astype(jnp.float32), k.astype(jnp.float32), v.astype(jnp.float32)
    qc = qf.reshape(B, nC, CHUNK, Hkv, G, d)

    def band(t):
        tp = jnp.pad(t, ((0, 0), ((W - 1) * CHUNK, 0)) + ((0, 0),) * (t.ndim - 2))
        tp = tp.reshape((B, nC + W - 1, CHUNK) + t.shape[2:])
        return jnp.concatenate([tp[:, w:w + nC] for w in range(W)], axis=2)

    k_band, v_band, pos_band = band(kf), band(vf), band(positions)
    pos_q = positions.reshape(B, nC, CHUNK)
    dist = jnp.abs(pos_q[..., :, None] - pos_band[..., None, :]).astype(jnp.float32)
    slopes = (2.0 ** (-8.0 * jnp.arange(1, Hq + 1, dtype=jnp.float32) / Hq)).reshape(Hkv, G)
    logits = jnp.einsum('bcqhgd,bckhd->bhgcqk', qc, k_band) / math.sqrt(d)
    logits = logits - slopes[None, :, :, None, None, None] * dist[:, None, None]
    c_idx = jnp.arange(nC, dtype=jnp.int32)[:, None]
    slot = jnp.arange(W * CHUNK, dtype=jnp.int32)[None, :] // CHUNK
    valid = (c_idx + slot - (W - 1)) >= 0
    logits = jnp.where(valid[None, None, None, :, None, :], logits, NEG_INF)
    sink_col = jnp.broadcast_to(sinks.astype(jnp.float32).reshape(Hkv, G)[None, :, :, None, None, None],
                                logits.shape[:-1] + (1,))
    p = jax.nn.softmax(jnp.concatenate([logits, sink_col], axis=-1), axis=-1)[..., :-1]
    out = jnp.einsum('bhgcqk,bckhd->bcqhgd', p, v_band)
    return out.reshape(B, S, Hq, d).astype(dtype)

def token_mixers(h, positions, w_in, q_norm_g, w_uq, kv_norm_g, w_ukv, sinks):
    B, S, _ = h.shape
    proj = h @ w_in
    split_points = [int(i) for i in np.cumsum(SPLIT_SIZES)[:-1]]
    qa, ka, va, cq, ckv, kr, qc, kc, vc = jnp.split(proj, split_points, axis=-1)

    o_a = stick_breaking_attention(qa.reshape(B, S, NH_A, HD_A), ka.reshape(B, S, NH_A, HD_A),
                                   va.reshape(B, S, NH_A, HD_A))

    q = (rms_norm(cq, q_norm_g) @ w_uq).reshape(B, S, NH_B, NOPE_B + ROPE_B)
    kv = (rms_norm(ckv, kv_norm_g) @ w_ukv).reshape(B, S, NH_B, NOPE_B + V_B)
    q_b = jnp.concatenate([q[..., :NOPE_B], rope(q[..., NOPE_B:], positions)], axis=-1)
    k_rope = jnp.broadcast_to(rope(kr[:, :, None, :], positions), (B, S, NH_B, ROPE_B))
    k_b = jnp.concatenate([kv[..., :NOPE_B], k_rope], axis=-1)
    o_b = chunk_causal_attention(q_b, k_b, kv[..., NOPE_B:])

    o_c = sliding_window_gqa(qc.reshape(B, S, NH_C, HD_C), kc.reshape(B, S, NKV_C, HD_C),
                             vc.reshape(B, S, NKV_C, HD_C), positions, sinks)

    return jnp.concatenate([o_a.reshape(B, S, -1), o_b.reshape(B, S, -1), o_c.reshape(B, S, -1)], axis=-1)

def setup_inputs(seed: int = 0) -> dict:
    key = jax.random.key(seed)
    ks = jax.random.split(key, 20)

    def nrm(k, shape, scale):
        return jax.random.normal(k, shape, jnp.float32) * scale

    offsets = jax.random.randint(ks[2], (BATCH,), 0, 16, dtype=jnp.int32) * CHUNK
    positions = jnp.arange(SEQ, dtype=jnp.int32)[None, :] + offsets[:, None]
    return {
        'x': nrm(ks[0], (BATCH, SEQ, D_MODEL), 1.0),
        'c': nrm(ks[1], (BATCH, D_MODEL), 1.0),
        'positions': positions,
        'ada_w': nrm(ks[3], (DEPTH, D_MODEL, 6 * D_MODEL), 0.1 * D_MODEL ** -0.5),
        'ada_b': nrm(ks[4], (DEPTH, 6 * D_MODEL), 0.01),
        'w_in': nrm(ks[5], (DEPTH, D_MODEL, IN_COLS), D_MODEL ** -0.5),
        'q_norm_g': 1.0 + nrm(ks[6], (DEPTH, Q_LORA), 0.01),
        'w_uq': nrm(ks[7], (DEPTH, Q_LORA, NH_B * (NOPE_B + ROPE_B)), Q_LORA ** -0.5),
        'kv_norm_g': 1.0 + nrm(ks[8], (DEPTH, KV_LORA), 0.01),
        'w_ukv': nrm(ks[9], (DEPTH, KV_LORA, NH_B * (NOPE_B + V_B)), KV_LORA ** -0.5),
        'sinks': nrm(ks[10], (DEPTH, NH_C), 0.5),
        'w_out': nrm(ks[11], (DEPTH, MIX, D_MODEL), BETA * MIX ** -0.5),
        'ln1_g': 1.0 + nrm(ks[12], (DEPTH, D_MODEL), 0.01),
        'ln1_b': nrm(ks[13], (DEPTH, D_MODEL), 0.01),
        'w_ff1': nrm(ks[14], (DEPTH, D_MODEL, D_FF), D_MODEL ** -0.5),
        'w_ff2': nrm(ks[15], (DEPTH, D_FF, D_MODEL), BETA * D_FF ** -0.5),
        'ln2_g': 1.0 + nrm(ks[16], (DEPTH, D_MODEL), 0.01),
        'ln2_b': nrm(ks[17], (DEPTH, D_MODEL), 0.01),
    }

def reference(x, c, positions, ada_w, ada_b, w_in, q_norm_g, w_uq, kv_norm_g, w_ukv, sinks,
              w_out, ln1_g, ln1_b, w_ff1, w_ff2, ln2_g, ln2_b):
    for l in range(DEPTH):
        mod = jax.nn.silu(c) @ ada_w[l] + ada_b[l]
        sh1, sc1, g1, sh2, sc2, g2 = jnp.split(mod[:, None, :], 6, axis=-1)
        h = x * (1.0 + sc1) + sh1
        mix = token_mixers(h, positions, w_in[l], q_norm_g[l], w_uq[l], kv_norm_g[l], w_ukv[l], sinks[l])
        x = layer_norm(ALPHA * x + (1.0 + g1) * (mix @ w_out[l]), ln1_g[l], ln1_b[l])
        h = x * (1.0 + sc2) + sh2
        f = jnp.square(jax.nn.relu(h @ w_ff1[l])) @ w_ff2[l]
        x = layer_norm(ALPHA * x + (1.0 + g2) * f, ln2_g[l], ln2_b[l])
    return x


_drawn_inputs = setup_inputs


def setup_inputs(seed=0):
    import zlib

    import numpy as np

    out = dict(_drawn_inputs(seed))
    spreads = {}
    factors = {'ada_b': 4.513,
     'q_norm_g': 8.0,
     'kv_norm_g': 8.0,
     'sinks': 8.0,
     'ln1_g': 3.924,
     'ln1_b': 3.635,
     'ln2_g': 4.052,
     'ln2_b': 3.797}
    for name, (base, spread) in spreads.items():
        noise = np.random.default_rng([zlib.crc32(name.encode()), seed]).standard_normal(out[name].shape)
        drawn = base * np.exp(spread * noise) if base else spread * noise
        out[name] = __import__('jax').numpy.asarray(drawn.astype(out[name].dtype))
    for name, factor in factors.items():
        out[name] = (out[name] * factor).astype(out[name].dtype)
    return out
```

```python
from contextlib import ExitStack

import numpy as np
import concourse.bass as bass
from concourse import mybir

F32 = mybir.dt.float32
F32R = mybir.dt.float32r
BF16 = mybir.dt.bfloat16
I32 = mybir.dt.int32
ALU = mybir.AluOpType
ACT = mybir.ActivationFunctionType
AXX = mybir.AxisListType.X

P = 128
S = 512
D = 1024
KT = D // P
DEPTH = 2
NT = S // P
CHUNK = 64
NH_A, NH_B, NH_C, HD = 4, 8, 4, 64
NOPE, ROPE = 64, 32
QK_B = NOPE + ROPE
Q_LORA, KV_LORA = 256, 128
D_FF = 4 * D
QUARTERS = 4
ALPHA = float((2 * DEPTH) ** 0.25)
LN_EPS = 1e-5
NEG = -1e30
FAR = 1e34
SLOPES = [2.0 ** (-8.0 * (h + 1) / NH_C) for h in range(NH_C)]
ITEM = 2048
CAUSAL = [S - P * j for j in range(NT)]
COFF = [sum(CAUSAL[:j]) for j in range(NT)]
KEYS = [P * (t + 1) for t in range(NT)]
KOFF = [sum(KEYS[:t]) for t in range(NT)]

P_UQ, P_OUT, P_FF = 7, 8, 12
PANELS = P_FF + 8 * QUARTERS
ORDER = ([("g", 0), ("g", 1), 2, ("g", 2), 3, 4, ("g", 3), 5, ("g", 4), 6, ("g", 5), 7, ("g", 6), ("g", 7), 8]
         + [("g", i) for i in range(8, 16)] + [("n", i) for i in range(8)]
         + [9, 10, 11, 12, 13] + list(range(14, PANELS + 2)))
PER_LAYER = len(ORDER)
FIRST_ITEMS = 10
RAW = 4
POS = {what: i for i, what in enumerate(ORDER)}
assert PER_LAYER % RAW == 0 and PER_LAYER == 68
TILES = 14 + NH_B + KT + 16 * QUARTERS
T_UQ, T_OUT, T_FF = 14, 14 + NH_B, 14 + NH_B + KT

V_ADAB, V_QG, V_KVG, V_LN1G, V_LN1B, V_LN2G, V_LN2B, V_SINK, NVEC = 0, 48, 50, 51, 59, 67, 75, 83, 88
C_ID, C_TRI, C_NEG1, C_M1024, C_M256, C_M128, C_FREQ, C_SIGN, C_EPS, C_ONE, C_ALPHA = \
    0, 128, 256, 384, 512, 640, 768, 769, 770, 771, 772
NCF = 776
DVE_LINKS = (0, 0, 0)
TWO_PI_PARTS = (6.28125, 0.0019350051879882812, 3.019916050561733e-07)


class Chain:

    def __init__(self, eng, sem):
        self.eng, self.sem, self.base, self.n = eng, sem, 0, 0

    def link(self, ins):
        self.n += 1
        ins.then_inc(self.sem, 1)
        self.eng.wait_ge(self.sem, self.base + self.n)


def build(nc, stream, ukv_d, x_d, vec_d, cT_d, pos_d, posq_d, cf_d, cb_d, maskc_d, out_d, links):
    ctx = ExitStack()
    with ctx:
        top = [(nc.sbuf_base + 31) // 32 * 32]

        def place(name, shape, dt, at=None):
            size = int(np.prod(shape[1:])) * (2 if dt == BF16 else 4)
            size = (size + 31) // 32 * 32
            if at is None:
                at = top[0]
                top[0] += size
            return nc.alloc_sbuf_tensor_at(name, shape, dt, offset=at), at + size

        def sb(name, shape, dt=F32):
            return place(name, shape, dt)[0]

        def sem(name):
            return ctx.enter_context(nc.semaphore(name))

        X = sb("X", [P, KT, S])
        HH = sb("HH", [P, KT, S], F32R)
        HL = sb("HL", [P, KT, S], F32R)
        raw = sb("raw", [P, RAW, ITEM])
        WH = sb("WH", [P, 2, ITEM], F32R)
        WL = sb("WL", [P, 2, ITEM], F32R)
        acc = sb("acc", [P, ITEM])
        UK = sb("UK", [P, 512])
        COS = sb("COS", [P, S])
        SIN = sb("SIN", [P, S])
        DIST = sb("DIST", [P, NT, 2 * P])
        CF = sb("CF", [P, NCF])
        CB = sb("CB", [P, 512], BF16)
        VEC = sb("VEC", [P, DEPTH + 1, NVEC])
        vec = sb("vec", [P, NVEC])
        modA = sb("modA", [P, 16])
        modB = sb("modB", [P, 32])
        g1p, g2p = sb("g1p", [P, 8]), sb("g2p", [P, 8])
        scp = sb("scp", [P, 8])
        gs1, bs1 = sb("gs1", [P, 8]), sb("bs1", [P, 8])
        gs2, bs2 = sb("gs2", [P, 8]), sb("bs2", [P, 8])
        cs = sb("cs", [P, KT])
        ce = sb("ce", [P, KT])
        mx = sb("mx", [P, 2, NT])
        nm = sb("nm", [P, 2, NT])
        den = sb("den", [P, 2, NT])
        esink = sb("esink", [P, 2, NT])
        rden = sb("rden", [P, 2, NT])
        CQH = sb("CQH", [P, 2, S], F32R)
        CQL = sb("CQL", [P, 2, S], F32R)
        shared = top[0]
        R = sb("R", [P, KT, S])
        FH = sb("FH", [P, KT, S], F32R)
        FL = sb("FL", [P, KT, S], F32R)
        end_shared = top[0]
        at = shared

        def over(name, shape, dt=F32):
            nonlocal at
            t, at = place(name, shape, dt, at)
            return t

        QB = over("QB", [P, 4, S])
        KB = over("KB", [P, 4, S])
        VB = over("VB", [P, NT, NH_B * HD])
        QA, KA = over("QA", [P, 2, S]), over("KA", [P, 2, S])
        VA = over("VA", [P, NT, NH_A * HD])
        QC, KC = over("QC", [P, 2, S]), over("KC", [P, S])
        VC = over("VC", [P, NT, 128])
        CKVN = over("CKVN", [P, S])
        UV = over("UV", [P, 512])
        assert at <= end_shared, (at, end_shared)
        work = top[0]
        W = [sb(f"W{i}", [P, 1280]) for i in range(3)]
        assert top[0] <= nc.sbuf_usable_end, (top[0], nc.sbuf_usable_end)
        at = work
        T = [over(f"T{i}", [P, S]) for i in range(7)]

        PS = ctx.enter_context(nc.psum_tensor("PS", [P, 8 * 512], F32))

        def bank(b, lo=0, hi=512):
            return PS[:, 512 * b + lo:512 * b + hi]

        raw_in = [sem(f"raw_in{i}") for i in range(RAW)]
        small_in = sem("small_in")
        x_in = sem("x_in")
        ukv_in = sem("ukv_in")
        out_done = sem("out_done")
        item_done = sem("item_done")
        hi_made = sem("hi_made")
        tile_done = sem("tile_done")
        hh_made, hl_made = sem("hh_made"), sem("hl_made")
        x_made = sem("x_made")
        modsum = sem("modsum")
        mods_made = sem("mods_made")
        dchain, achain = sem("dchain"), sem("achain")
        silu_e = sem("silu_e")
        trig_in, trig_made = sem("trig_in"), sem("trig_made")
        silu_made = sem("silu_made")
        sq_made = sem("sq_made")
        ssq_made = sem("ssq_made")
        rs_exp = sem("rs_exp")
        cq_made, cqh_made, cql_made = sem("cq_made"), sem("cqh_made"), sem("cql_made")
        dve_evac, act_evac = sem("dve_evac"), sem("act_evac")
        vb_made = sem("vb_made")
        vbp_made = sem("vbp_made")
        z_made, az_made, ln_made, sp_made = sem("z_made"), sem("az_made"), sem("ln_made"), sem("sp_made")
        ex_made, w_made = sem("ex_made"), sem("w_made")
        o_made, oh_made, ol_made = sem("o_made"), sem("oh_made"), sem("ol_made")
        kp_made, kn_made, krope_made = sem("kp_made"), sem("kn_made"), sem("krope_made")
        qn_made, qr_made = sem("qn_made"), sem("qr_made")
        s_made, nm_made, p_made, pn_made = sem("s_made"), sem("nm_made"), sem("p_made"), sem("pn_made")
        pt_made, ptc_made, pta_made, ptd_made = sem("pt_made"), sem("ptc_made"), sem("pta_made"), sem("ptd_made")
        sc_made, nmc_made, pc_made, pnc_made = sem("sc_made"), sem("nmc_made"), sem("pc_made"), sem("pnc_made")
        r_init = sem("r_init")
        r_made = sem("r_made")
        mean_made, dif_made, lsq_made, var_part = sem("mean_made"), sem("dif_made"), sem("lsq_made"), sem("var_part")
        var_exp = sem("var_exp")
        xn_made = sem("xn_made")
        relu_made, fh_made, fl_made, ft_read = sem("relu_made"), sem("fh_made"), sem("fl_made"), sem("ft_read")

        ident = CF[:, C_ID:C_ID + P]
        block = ctx.enter_context(nc.Block())

        def raw_count(i, l=None, q=0):
            n = 16 * ((FIRST_ITEMS + i) // RAW + 1)
            return n if l is None else l * (16 * PER_LAYER // RAW) + q * (16 * 8 // RAW) + n

        def raw_slot(i):
            return (FIRST_ITEMS + i) % RAW

        B_ORDER = (0, 2, 1, 3)

        def b_scores(t):
            b, lo = ((1, 384), (2, 0), (1, 0), (0, 0))[t]
            return bank(b, lo, lo + KEYS[t])

        @block.sync
        def _(sp):
            sp.dma_start(cs[:, :], cT_d).then_inc(small_in, 16)
            sp.dma_start(VEC[:, :, :], vec_d).then_inc(small_in, 16)
            sp.dma_start(CF[:, :], cf_d).then_inc(small_in, 16)
            sp.dma_start(CB[:, :], cb_d).then_inc(small_in, 16)
            sp.dma_start(T[0][:, :].bitcast(I32), pos_d.to_broadcast([P, S])).then_inc(small_in, 16)
            sp.dma_start(mx[:, 0, :].bitcast(I32), posq_d).then_inc(small_in, 16)
            sp.dma_start(T[3][:, 0:2 * P], maskc_d).then_inc(small_in, 16)
            total = FIRST_ITEMS + DEPTH * PER_LAYER
            for n in range(RAW):
                sp.dma_start(raw[:, n, :], stream[n, :, :]).then_inc(raw_in[n], 16)
            sp.dma_start(X[:, :, :], x_d).then_inc(x_in, 16)
            rest = (total - RAW) % RAW
            with sp.Fori(0, (total - rest) // RAW - 1) as g:
                for k in range(RAW):
                    sp.wait_ge(item_done, g * RAW + k + 1)
                    sp.dma_start(raw[:, k, :], stream[bass.ds(g * RAW + RAW + k, 1), :, :].rearrange("a p n -> (a p) n"))\
                      .then_inc(raw_in[k], 16)
            for n in range(total - rest, total):
                sp.wait_ge(item_done, n - RAW + 1)
                sp.dma_start(raw[:, n % RAW, :], stream[n, :, :]).then_inc(raw_in[n % RAW], 16)
            sp.wait_ge(x_made, 16 * DEPTH)
            sp.dma_start(out_d, X[:, :, :]).then_inc(out_done, 16)
            sp.wait_ge(out_done, 16)

        @block.gpsimd
        def _(pool):
            alpha = CF[:, C_ALPHA:C_ALPHA + 1].to_broadcast([P, S])
            pool.wait_ge(small_in, 16 * 7)
            with pool.Fori(0, DEPTH) as l:
                pool.wait_ge(o_made, l * 16 + 16)
                pool.wait_ge(oh_made, l * 16 + 16)
                pool.wait_ge(ol_made, l * 16 + 16)
                for o in range(KT):
                    pool.tensor_tensor(R[:, o, :], X[:, o, :], alpha, ALU.mult).then_inc(r_init, 1)
                for o in range(KT):
                    pool.wait_ge(x_made, l * 16 + o + 1)
                    pool.wait_ge(hl_made, l * 16 + 8 + o + 1)
                    pool.tensor_tensor(R[:, o, :], X[:, o, :], alpha, ALU.mult).then_inc(r_init, 1)

        @block.scalar
        def _(act):
            chain = Chain(act, achain)
            link = chain.link
            eps = CF[:, C_EPS:C_EPS + 1]

            def high(n, l=None, q=0):
                i = POS.get(n)
                if l is None:
                    i = n - 2
                    act.wait_ge(raw_in[raw_slot(i)], raw_count(i))
                else:
                    act.wait_ge(raw_in[raw_slot(i)], raw_count(i, l, q))
                    free = 2 * (n - 1) if n < 9 else T_OUT + 2 * (n - 9) if n > 9 else T_OUT
                    act.wait_ge(tile_done, l * TILES + q * 16 + free)
                act.activation(WH[:, n % 2, :], raw[:, raw_slot(i), :], ACT.Copy).then_inc(hi_made, 1)

            def h_high(o, src, g, b, inc=hh_made):
                act.activation(HH[:, o, :], src, ACT.Identity, scale=g[:, o:o + 1], bias=b[:, o:o + 1])\
                   .then_inc(inc, 1)

            act.wait_ge(small_in, 16 * 7)
            act.activation(ce[:, :], cs[:, :], ACT.Exp, scale=-1.0).then_inc(silu_e, 1)
            act.wait_ge(trig_in, 1)
            act.activation(SIN[:, :], T[1][:, :], ACT.Sin).then_inc(trig_made, 1)
            act.wait_ge(trig_in, 2)
            act.activation(COS[:, :], T[2][:, :], ACT.Sin).then_inc(trig_made, 1)
            high(0)
            high(1)
            act.wait_ge(x_in, 16)
            act.wait_ge(mods_made, 1)
            for o in range(KT):
                h_high(o, X[:, o, :], gs2, bs2)

            def layer_norm_act(l, which):
                n0 = 8 * which
                for o in range(KT):
                    act.wait_ge(dif_made, l * 16 + n0 + o + 1)
                    if o >= 3:
                        act.wait_ge(var_part, l * 16 + n0 + o - 2)
                    act.activation(T[o % 3][:, :], R[:, o, :], ACT.Square).then_inc(lsq_made, 1)
                act.wait_ge(var_part, l * 16 + n0 + 8)
                link(act.activation(T[3][:, :], bank(7), ACT.Ln, bias=eps))
                act.activation(T[4][:, :], T[3][:, :], ACT.Exp, scale=-0.5).then_inc(var_exp, 1)
                g, b = ((gs1, bs1), (gs2, bs2))[which]
                vg = (V_LN1G, V_LN2G)[which]
                vb = (V_LN1B, V_LN2B)[which]
                for o in range(KT):
                    act.wait_ge(xn_made, l * 16 + n0 + o + 1)
                    h_high(o, R[:, o, :], g, b)
                    act.activation(X[:, o, :], R[:, o, :], ACT.Identity, scale=vec[:, vg + o:vg + o + 1],
                                   bias=vec[:, vb + o:vb + o + 1]).then_inc(x_made, 1)

            n_start = chain.n
            with act.Fori(0, DEPTH) as l:
                chain.base, chain.n = n_start + l * links["act"], 0

                def tile(n):
                    act.wait_ge(tile_done, l * TILES + n)

                act.wait_ge(hl_made, l * 16 + 8)
                ukv = ukv_d[bass.ds(l, 1), :, :].rearrange("a p n -> (a p) n")
                act.dma_start(UK[:, :], ukv[:, 0:512]).then_inc(ukv_in, 16)
                act.dma_start(UV[:, :], ukv[:, 512:1024]).then_inc(ukv_in, 16)
                tile(1)
                act.activation(T[0][:, :], bank(0), ACT.Square).then_inc(sq_made, 1)
                tile(2)
                act.activation(T[1][:, :], bank(1), ACT.Square).then_inc(sq_made, 1)
                high(2, l)
                tile(3)
                act.activation(T[2][:, :], bank(2), ACT.Square).then_inc(sq_made, 1)
                high(3, l)
                act.wait_ge(ssq_made, l * 2 + 1)
                link(act.activation(T[3][:, :], bank(6), ACT.Ln, bias=eps))
                act.activation(T[4][:, :], T[3][:, :], ACT.Exp, scale=-0.5).then_inc(rs_exp, 1)
                tile(5)
                act.activation(QA[:, 0, :], bank(4), ACT.Copy, scale=HD ** -0.5).then_inc(act_evac, 1)
                for k in range(2):
                    act.wait_ge(cq_made, l * 2 + k + 1)
                    act.activation(CQH[:, k, :], T[k][:, :], ACT.Copy).then_inc(cqh_made, 1)
                tile(6)
                act.activation(QA[:, 1, :], bank(5), ACT.Copy, scale=HD ** -0.5).then_inc(act_evac, 1)
                high(4, l)
                act.wait_ge(ssq_made, l * 2 + 2)
                link(act.activation(T[5][:, :], bank(7), ACT.Ln, bias=eps))
                act.activation(T[6][:, :], T[5][:, :], ACT.Exp, scale=-0.5).then_inc(rs_exp, 1)
                high(5, l)
                tile(9)
                act.activation(QC[:, 0, :], bank(2), ACT.Copy, scale=HD ** -0.5).then_inc(act_evac, 1)
                tile(10)
                act.activation(QC[:, 1, :], bank(3), ACT.Copy, scale=HD ** -0.5).then_inc(act_evac, 1)
                high(6, l)
                high(7, l)
                high(8, l)
                for t in range(2):
                    act.wait_ge(vbp_made, l * 4 + t + 1)
                    act.activation(VB[:, t, :], bank(4 + t), ACT.Copy).then_inc(vb_made, 1)

                def soft(h):
                    for j in reversed(range(NT)):
                        w = W[h % 2][:, COFF[j]:COFF[j] + CAUSAL[j]]
                        act.wait_ge(az_made, l * 16 + 4 * h + NT - j)
                        e = act.activation(w, w, ACT.Exp, scale=-1.0)
                    link(e)
                    for j in reversed(range(NT)):
                        w = W[h % 2][:, COFF[j]:COFF[j] + CAUSAL[j]]
                        act.activation(w, w, ACT.Ln, bias=CF[:, C_ONE:C_ONE + 1]).then_inc(ln_made, 1)

                def weights(h):
                    if h >= 1:
                        act.wait_ge(o_made, l * 16 + h)
                    for i in reversed(range(NT)):
                        act.wait_ge(ex_made, l * 16 + 4 * h + NT - i)
                        act.activation(W[2][:, COFF[i]:COFF[i] + CAUSAL[i]],
                                       bank(4 * (h % 2) + i, 0, CAUSAL[i]), ACT.Exp).then_inc(w_made, 1)

                def mixed_high(u, b, row, tl):
                    act.wait_ge(o_made, l * 16 + u + 1)
                    act.activation(HH[row:row + HD, tl, :], PS[row:row + HD, 512 * b:512 * b + 512], ACT.Copy)\
                       .then_inc(oh_made, 1)

                soft(0)
                soft(1)
                for h in (0, 2):
                    weights(h)
                    weights(h + 1)
                    for k in (h, h + 1):
                        mixed_high(k, 4 * (k % 2) + 3, HD * (k % 2), k // 2)
                        if h == 0:
                            soft(k + 2)

                def key_nope(pr):
                    act.wait_ge(kp_made, l * 4 + pr + 1)
                    for k in range(2):
                        if pr >= 2:
                            act.wait_ge(s_made, l * 32 + 4 * (2 * pr + k - 4 + 1))
                        act.activation(KB[0:NOPE, (2 * pr + k) % 4, :],
                                       PS[NOPE * k:NOPE * (k + 1), 512 * 7:512 * 8], ACT.Copy).then_inc(kn_made, 1)

                def query_nope(h):
                    tile(T_UQ + h + 1)
                    act.activation(QB[0:NOPE, h % 4, :], PS[0:NOPE, 512 * 7:512 * 8], ACT.Copy).then_inc(qn_made, 1)

                key_nope(0)
                query_nope(0)
                for h in range(NH_B):
                    if h + 1 < NH_B:
                        if (h + 1) % 2 == 0:
                            key_nope((h + 1) // 2)
                        query_nope(h + 1)
                    if h >= 2:
                        act.wait_ge(pt_made, l * 8 + h - 1)
                    act.wait_ge(nm_made, l * 8 + h + 1)
                    for t in range(NT):
                        act.activation(W[h % 2][:, KOFF[t]:KOFF[t] + KEYS[t]], b_scores(t), ACT.Exp,
                                       bias=nm[:, h % 2, t:t + 1], scale=QK_B ** -0.5,
                                       accum_out=den[:, h % 2, t:t + 1]).then_inc(p_made, 1)
                    act.wait_ge(pt_made, l * 8 + h + 1)
                    act.activation(W[2][:, 0:512], bank(3), ACT.Copy).then_inc(pta_made, 1)
                    act.activation(W[2][:, 896:1152], bank(5, 0, 256), ACT.Copy).then_inc(pta_made, 1)
                    mixed_high(4 + h, 6, HD * (h % 2), 2 + h // 2)
                high(9, l)

                for c in range(NH_C):
                    act.wait_ge(nmc_made, l * 4 + c + 1)
                    wv = W[c % 2][:, 0:1024].rearrange("p (t k) -> p t k", t=NT)
                    for t in range(NT):
                        act.activation(wv[:, t, :], wv[:, t, :], ACT.Exp, bias=nm[:, c % 2, t:t + 1],
                                       accum_out=den[:, c % 2, t:t + 1]).then_inc(pc_made, 1)
                    act.activation(esink[:, c % 2, :], nm[:, c % 2, :], ACT.Exp,
                                   bias=vec[:, V_SINK + c:V_SINK + c + 1]).then_inc(pc_made, 1)
                    act.wait_ge(ptc_made, l * 4 + c + 1)
                    act.activation(W[2][:, 0:512], bank(4), ACT.Copy).then_inc(pta_made, 1)
                    mixed_high(12 + c, 6, HD * (c % 2), 6 + c // 2)

                for n in range(P_OUT, P_FF):
                    high(n + 2, l)
                layer_norm_act(l, 0)

                with act.Fori(0, QUARTERS) as q:
                    base = chain.base
                    n_before = chain.n
                    for j in range(8):
                        n = P_FF + j
                        if j < 4:
                            for t in range(2):
                                u = 2 * j + t
                                act.wait_ge(tile_done, l * TILES + q * 16 + T_FF + u + 1)
                                if u >= 2:
                                    act.wait_ge(fl_made, l * 32 + q * 8 + u - 1)
                                act.activation(T[u % 2][:, :], bank(u % 4), ACT.Relu).then_inc(relu_made, 1)
                                act.wait_ge(relu_made, l * 32 + q * 8 + u + 1)
                                act.activation(FH[:, u, :], T[u % 2][:, :], ACT.Square).then_inc(fh_made, 1)
                        high(n + 2, l, q)
                layer_norm_act(l, 1)
                assert chain.n == links["act"], ("act", chain.n)

        @block.vector
        def _(dve):
            chain = Chain(dve, dchain)
            link = chain.link
            tt, ts, stt = dve.tensor_tensor, dve.tensor_scalar, dve.scalar_tensor_tensor

            def magnitude(out, x):
                return ts(out.bitcast(I32), x.bitcast(I32), 0x7fffffff, None, ALU.bitwise_and)

            def low(n, l=None, q=0):
                i = POS.get(n) if l is not None else n - 2
                if l is None:
                    dve.wait_ge(hi_made, n + 1)
                else:
                    dve.wait_ge(hi_made, l * PANELS + q * 8 + n + 1)
                tt(WL[:, n % 2, :], raw[:, raw_slot(i), :], WH[:, n % 2, :].bitcast(F32), ALU.subtract)\
                    .then_inc(item_done, 1)

            def modulate(i, kt, l=None):
                if l is None:
                    dve.wait_ge(raw_in[raw_slot(i)], raw_count(i))
                else:
                    dve.wait_ge(raw_in[raw_slot(i)], raw_count(i, l))
                src = raw[:, raw_slot(i), :]
                if kt == 0:
                    ts(acc[:, :], src, cs[:, 0:1], None, ALU.mult).then_inc(item_done, 1)
                else:
                    if l is None:
                        dve.wait_ge(item_done, i + FIRST_ITEMS)
                    else:
                        dve.wait_ge(item_done, l * PER_LAYER + (i + FIRST_ITEMS))
                    stt(acc[:, :], src, cs[:, kt:kt + 1], acc[:, :], ALU.mult, ALU.add).then_inc(item_done, 1)

            def h_low(o, src, g, b, n):
                t = T[5 + o % 2]
                link(ts(t[:, :], src, g[:, o:o + 1], b[:, o:o + 1], ALU.mult, ALU.add))
                dve.wait_ge(hh_made, n)
                tt(HL[:, o, :], t[:, :], HH[:, o, :].bitcast(F32), ALU.subtract).then_inc(hl_made, 1)

            dve.wait_ge(silu_e, 1)
            link(ts(ce[:, :], ce[:, :], 1.0, None, ALU.add))
            link(dve.reciprocal(ce[:, :], ce[:, :]))
            link(tt(cs[:, :], cs[:, :], ce[:, :], ALU.mult))
            magic = 12582912.0
            link(dve.tensor_copy(T[4][:, :], T[0][:, :].bitcast(I32)))
            link(dve.tensor_copy(mx[:, 1, :], mx[:, 0, :].bitcast(I32)))
            link(ts(T[5][:, :], T[4][:, :], CF[:, C_FREQ:C_FREQ + 1], None, ALU.mult))
            for k, quarter in enumerate((0.0, 0.25)):
                link(ts(T[0][:, :], T[5][:, :], float(1 / (2 * np.pi)), quarter, ALU.mult, ALU.add))
                link(ts(T[0][:, :], T[0][:, :], magic, None, ALU.add))
                link(ts(T[0][:, :], T[0][:, :], magic, None, ALU.subtract))
                r = T[1 + k]
                link(stt(r[:, :], T[0][:, :], -TWO_PI_PARTS[0], T[5][:, :], ALU.mult, ALU.add))
                link(stt(r[:, :], T[0][:, :], -TWO_PI_PARTS[1], r[:, :], ALU.mult, ALU.add))
                link(stt(r[:, :], T[0][:, :], -TWO_PI_PARTS[2], r[:, :], ALU.mult, ALU.add))
                if k:
                    link(ts(r[:, :], r[:, :], float(np.pi / 2), None, ALU.add))
                ts(r[:, :], r[:, :], 3.1415925, -3.1415925, ALU.min, ALU.max).then_inc(trig_in, 1)
            for t in range(NT):
                lo = P * max(t - 1, 0)
                dst = DIST[:, t, P:2 * P] if t == 0 else DIST[:, t, :]
                n = P if t == 0 else 2 * P
                link(ts(dst, T[4][:, lo:lo + n], mx[:, 1, t:t + 1], None, ALU.subtract))
                link(magnitude(dst, dst))
                link(tt(dst, dst, T[3][:, 2 * P - n:2 * P], ALU.add))
            link(dve.memset(DIST[:, 0, 0:P], FAR))
            link(dve.tensor_copy(vec[:, :], VEC[:, 0, :]))
            dve.wait_ge(trig_made, 2)
            link(ts(SIN[:, :], SIN[:, :], CF[:, C_SIGN:C_SIGN + 1], None, ALU.mult))
            for kt in range(KT):
                modulate(kt - FIRST_ITEMS, kt)
            low(0)
            low(1)
            dve.wait_ge(modsum, 1)
            link(tt(modA[:, :], bank(0, 0, 16), VEC[:, 0, 0:16], ALU.add))
            link(dve.tensor_copy(bs2[:, :], modA[:, 0:8]))
            ts(gs2[:, :], modA[:, 8:16], 1.0, None, ALU.add).then_inc(mods_made, 1)
            dve.wait_ge(mods_made, 1)
            dve.wait_ge(x_in, 16)
            for o in range(KT):
                h_low(o, X[:, o, :], gs2, bs2, o + 1)

            def layer_norm_dve(l, which):
                n0 = 8 * which
                dve.wait_ge(mean_made, l * 2 + which + 1)
                for o in range(KT):
                    tt(R[:, o, :], R[:, o, :], bank(6), ALU.subtract).then_inc(dif_made, 1)
                dve.wait_ge(var_exp, l * 2 + which + 1)
                link(tt(T[3][:, :], T[4][:, :], T[4][:, :], ALU.mult))
                link(stt(T[3][:, :], bank(7), LN_EPS, T[3][:, :], ALU.add, ALU.mult))
                link(ts(T[3][:, :], T[3][:, :], -0.5, 1.5, ALU.mult, ALU.add))
                link(tt(T[4][:, :], T[3][:, :], T[4][:, :], ALU.mult))
                g, b = ((gs1, bs1), (gs2, bs2))[which]
                for o in range(KT):
                    tt(R[:, o, :], R[:, o, :], T[4][:, :], ALU.mult).then_inc(xn_made, 1)
                    dve.wait_ge(xn_made, l * 16 + n0 + o + 1)
                    h_low(o, R[:, o, :], g, b, l * 16 + 8 + n0 + o + 1)

            def rms_factor(l, k, y, t, b):
                dve.wait_ge(rs_exp, l * 2 + k + 1)
                link(tt(t[:, :], y[:, :], y[:, :], ALU.mult))
                link(stt(t[:, :], bank(b), LN_EPS, t[:, :], ALU.add, ALU.mult))
                link(ts(t[:, :], t[:, :], -0.5, 1.5, ALU.mult, ALU.add))
                link(tt(y[:, :], t[:, :], y[:, :], ALU.mult))

            n_start = chain.n
            with dve.Fori(0, DEPTH) as l:
                chain.base, chain.n = n_start + l * links["dve"], 0

                def tile(n):
                    dve.wait_ge(tile_done, l * TILES + n)

                def own(i):
                    modulate(POS["g", i], i % KT, l)

                def following(i):
                    modulate(POS["n", i], i, l)

                own(0)
                own(1)
                low(2, l)
                own(2)
                low(3, l)
                tile(4)
                link(tt(KA[NOPE:QK_B, 0, :], PS[NOPE:QK_B, 512 * 3:512 * 4], COS[NOPE:QK_B, :], ALU.mult))
                link(tt(KA[NOPE:QK_B, 1, :], PS[QK_B:P, 512 * 3:512 * 4], SIN[QK_B:P, :], ALU.mult))
                for k in range(4):
                    tt(KB[NOPE:QK_B, k, :], KA[NOPE:QK_B, 0, :], KA[NOPE:QK_B, 1, :], ALU.add)\
                        .then_inc(krope_made, 1)
                rms_factor(l, 0, T[4], T[3], 6)
                for k in range(2):
                    stt(T[k][:, :], bank(k), vec[:, V_QG + k:V_QG + k + 1], T[4][:, :], ALU.mult, ALU.mult)\
                        .then_inc(cq_made, 1)
                for k in range(2):
                    dve.wait_ge(cqh_made, l * 2 + k + 1)
                    tt(CQL[:, k, :], T[k][:, :], CQH[:, k, :].bitcast(F32), ALU.subtract).then_inc(cql_made, 1)
                low(4, l)
                rms_factor(l, 1, T[6], T[5], 7)
                stt(CKVN[:, :], bank(2), vec[:, V_KVG:V_KVG + 1], T[6][:, :], ALU.mult, ALU.mult)\
                    .then_inc(dve_evac, 1)
                own(3)
                low(5, l)
                for k in range(2):
                    tile(7 + k)
                    dve.tensor_copy(KA[:, k, :], bank(k)).then_inc(dve_evac, 1)
                own(4)
                low(6, l)
                own(5)
                low(7, l)
                tile(11)
                dve.tensor_copy(KC[:, :], bank(4)).then_inc(dve_evac, 1)
                tile(12)
                dve.tensor_copy(VC[:, :, :], bank(5).rearrange("p (t n) -> p t n", t=NT)).then_inc(dve_evac, 1)
                own(6)
                own(7)
                for k in range(2):
                    tile(13 + k)
                    dve.tensor_copy(VA[:, 2 * k:2 * k + 2, :], bank(k).rearrange("p (t n) -> p t n", t=2))\
                        .then_inc(dve_evac, 1)
                low(8, l)
                for t in range(2, 4):
                    dve.wait_ge(vbp_made, l * 4 + t + 1)
                    dve.tensor_copy(VB[:, t, :], bank(4 + t)).then_inc(vb_made, 1)
                dve.wait_ge(modsum, l * 3 + 2)
                tt(modB[:, 0:16], bank(0, 0, 16), vec[:, 16:32], ALU.add).then_inc(mods_made, 1)
                dve.wait_ge(mods_made, l * 3 + 2)
                link(ts(g1p[:, :], modB[:, 0:8], 1.0, None, ALU.add))

                def absolute(h):
                    for j in reversed(range(NT)):
                        dve.wait_ge(z_made, l * 16 + 4 * h + NT - j)
                        magnitude(W[h % 2][:, COFF[j]:COFF[j] + CAUSAL[j]], bank(4 * (h % 2) + j, 0, CAUSAL[j]))\
                            .then_inc(az_made, 1)

                def softplus(h):
                    for j in reversed(range(NT)):
                        dve.wait_ge(ln_made, l * 16 + 4 * h + NT - j)
                        w = W[h % 2][:, COFF[j]:COFF[j] + CAUSAL[j]]
                        stt(w, bank(4 * (h % 2) + j, 0, CAUSAL[j]), 0.0, w, ALU.max, ALU.add).then_inc(sp_made, 1)

                def mixed_low(u, b, row, tl):
                    dve.wait_ge(oh_made, l * 16 + u + 1)
                    tt(HL[row:row + HD, tl, :], PS[row:row + HD, 512 * b:512 * b + 512],
                       HH[row:row + HD, tl, :].bitcast(F32), ALU.subtract).then_inc(ol_made, 1)

                absolute(0)
                absolute(1)
                softplus(0)
                softplus(1)
                for h in range(NH_A):
                    own(8 + 2 * h)
                    own(9 + 2 * h)
                    mixed_low(h, 4 * (h % 2) + 3, HD * (h % 2), h // 2)
                    if h + 2 < NH_A:
                        absolute(h + 2)
                        softplus(h + 2)

                def query_rope(h):
                    tile(T_UQ + h + 1)
                    link(tt(rope_tmp(0), PS[NOPE:QK_B, 512 * 7:512 * 8], COS[NOPE:QK_B, :], ALU.mult))
                    link(tt(rope_tmp(1), PS[QK_B:P, 512 * 7:512 * 8], SIN[QK_B:P, :], ALU.mult))
                    tt(QB[NOPE:QK_B, h % 4, :], rope_tmp(0), rope_tmp(1), ALU.add).then_inc(qr_made, 1)

                def rope_tmp(k):
                    return QA[NOPE:QK_B, k, :]

                query_rope(0)
                dve.wait_ge(modsum, l * 3 + 3)
                tt(modB[:, 16:32], bank(3, 0, 16), vec[:, 32:48], ALU.add).then_inc(mods_made, 1)
                dve.wait_ge(mods_made, l * 3 + 3)
                link(ts(scp[:, :], modB[:, 16:24], 1.0, None, ALU.add))
                link(ts(g2p[:, :], modB[:, 24:32], 1.0, None, ALU.add))
                link(tt(gs1[:, :], vec[:, V_LN1G:V_LN1G + 8], scp[:, :], ALU.mult))
                link(tt(bs1[:, :], vec[:, V_LN1B:V_LN1B + 8], scp[:, :], ALU.mult))
                link(tt(bs1[:, :], bs1[:, :], modB[:, 8:16], ALU.add))
                for h in range(NH_B):
                    for k, t in enumerate(B_ORDER):
                        dve.wait_ge(s_made, l * 32 + 4 * h + max(k, 1) + 1)
                        m = dve.reduce_max(mx[:, h % 2, t:t + 1], b_scores(t), axis=AXX)
                    link(m)
                    ts(nm[:, h % 2, :], mx[:, h % 2, :], -(QK_B ** -0.5), None, ALU.mult).then_inc(nm_made, 1)
                    if h + 1 < NH_B:
                        query_rope(h + 1)
                    following(h)
                    dve.wait_ge(p_made, l * 32 + 4 * h + 4)
                    link(dve.reciprocal(rden[:, h % 2, :], den[:, h % 2, :]))
                    for t in range(NT):
                        w = W[h % 2][:, KOFF[t]:KOFF[t] + KEYS[t]]
                        ts(w, w, rden[:, h % 2, t:t + 1], None, ALU.mult).then_inc(pn_made, 1)
                    dve.wait_ge(pt_made, l * 8 + h + 1)
                    dve.tensor_copy(W[2][:, 512:896], bank(4, 0, 384)).then_inc(ptd_made, 1)
                    dve.tensor_copy(W[2][:, 1152:1280], bank(4, 384, 512)).then_inc(ptd_made, 1)
                    mixed_low(4 + h, 6, HD * (h % 2), 2 + h // 2)
                dve.wait_ge(modsum, l * 3 + 4)
                tt(modA[:, :], bank(7, 0, 16), VEC[:, bass.ds(l + 1, 1), 0:16].rearrange("p a n -> p (a n)"), ALU.add)\
                    .then_inc(mods_made, 1)
                dve.wait_ge(mods_made, l * 3 + 4)
                link(ts(scp[:, :], modA[:, 8:16], 1.0, None, ALU.add))
                link(tt(gs2[:, :], vec[:, V_LN2G:V_LN2G + 8], scp[:, :], ALU.mult))
                link(tt(bs2[:, :], vec[:, V_LN2B:V_LN2B + 8], scp[:, :], ALU.mult))
                link(tt(bs2[:, :], bs2[:, :], modA[:, 0:8], ALU.add))
                low(9, l)

                def window_logits(c):
                    dve.wait_ge(sc_made, l * 4 + c + 1)
                    wv = W[c % 2][:, 0:1024].rearrange("p (t k) -> p t k", t=NT)
                    if c >= 2:
                        dve.wait_ge(ptc_made, l * 4 + c - 1)
                    link(stt(W[c % 2][:, 0:1024], DIST[:, :, :].rearrange("p t k -> p (t k)"), -SLOPES[c],
                             PS[:, 1024 * (c % 2):1024 * (c % 2) + 1024], ALU.mult, ALU.add))
                    link(dve.reduce_max(mx[:, c % 2, :], wv, axis=AXX))
                    ts(nm[:, c % 2, :], mx[:, c % 2, :], vec[:, V_SINK + c:V_SINK + c + 1], -1.0, ALU.max, ALU.mult)\
                        .then_inc(nmc_made, 1)

                window_logits(0)
                for c in range(NH_C):
                    wv = W[c % 2][:, 0:1024].rearrange("p (t k) -> p t k", t=NT)
                    if c + 1 < NH_C:
                        window_logits(c + 1)
                    dve.wait_ge(pc_made, l * 20 + 5 * c + 5)
                    link(tt(den[:, c % 2, :], den[:, c % 2, :], esink[:, c % 2, :], ALU.add))
                    link(dve.reciprocal(rden[:, c % 2, :], den[:, c % 2, :]))
                    for t in range(NT):
                        ts(wv[:, t, :], wv[:, t, :], rden[:, c % 2, t:t + 1], None, ALU.mult).then_inc(pnc_made, 1)
                    dve.wait_ge(ptc_made, l * 4 + c + 1)
                    dve.tensor_copy(W[2][:, 512:896], bank(5, 0, 384)).then_inc(ptd_made, 1)
                    mixed_low(12 + c, 6, HD * (c % 2), 6 + c // 2)

                for n in range(P_OUT, P_FF):
                    for t in range(2):
                        o = 2 * (n - P_OUT) + t
                        tile(T_OUT + o + 1)
                        dve.wait_ge(r_init, l * 16 + o + 1)
                        stt(R[:, o, :], bank(o % 4), g1p[:, o:o + 1], R[:, o, :], ALU.mult, ALU.add).then_inc(r_made, 1)
                    low(n + 2, l)
                layer_norm_dve(l, 0)

                n_before = chain.n
                with dve.Fori(0, QUARTERS) as q:
                    chain_base = chain.base
                    chain.base = chain_base + q * links["dve_q"]
                    for j in range(8):
                        n = P_FF + j
                        for t in range(2):
                            u = 2 * (j % 4) + t
                            if j < 4:
                                dve.wait_ge(relu_made, l * 32 + q * 8 + u + 1)
                                link(tt(T[2 + u % 2][:, :], T[u % 2][:, :], T[u % 2][:, :], ALU.mult))
                                dve.wait_ge(fh_made, l * 32 + q * 8 + u + 1)
                                tt(FL[:, u, :], T[2 + u % 2][:, :], FH[:, u, :].bitcast(F32), ALU.subtract)\
                                    .then_inc(fl_made, 1)
                            else:
                                dve.wait_ge(tile_done, l * TILES + q * 16 + T_FF + 8 + u + 1)
                                if u == 0:
                                    dve.wait_ge(r_init, l * 16 + 16)
                                dve.wait_ge(r_made, l * 40 + q * 8 + 8)
                                stt(R[:, u, :], bank(u % 4), g2p[:, u:u + 1], R[:, u, :], ALU.mult, ALU.add)\
                                    .then_inc(r_made, 1)
                        low(n + 2, l, q)
                    assert chain.n - n_before == links["dve_q"], ("dve_q", chain.n - n_before)
                chain.base = chain_base
                chain.n = n_before + QUARTERS * links["dve_q"]
                layer_norm_dve(l, 1)
                dve.wait_ge(x_made, l * 16 + 16)
                link(ts(vec[:, :], VEC[:, bass.ds(l + 1, 1), :].rearrange("p a n -> p (a n)"), 1.0, None, ALU.mult))
                assert chain.n == links["dve"], ("dve", chain.n)

        @block.tensor
        def _(pe):
            mm = pe.matmul

            def panel_made(n, l, q=0):
                at = FIRST_ITEMS + (POS[n] if n >= 2 else n - 2)
                pe.wait_ge(item_done, l * PER_LAYER + q * 8 + at + 1)

            def product(out, pairs, first=True, last=True):
                for k, (wh, wl, xh, xl) in enumerate(pairs):
                    mm(out, wh, xh, start=first and k == 0, stop=False)
                    mm(out, wh, xl, start=False, stop=False)
                    m = mm(out, wl, xh, start=False, stop=last and k == len(pairs) - 1)
                return m

            def modulation_sum(b):
                for c in range(ITEM // P):
                    m = mm(bank(b, c, c + 1), acc[:, c * P:(c + 1) * P], CF[:, C_ONE:C_ONE + 1], start=True, stop=True)
                m.then_inc(modsum, 1)

            pe.wait_ge(small_in, 16 * 7)
            pe.wait_ge(item_done, 8)
            modulation_sum(0)

            def layer_norm_pe(l, which, interleaved=False):
                n0 = 8 * which
                if not interleaved:
                    for o in range(KT):
                        mean_step(l, which, o)
                for o in range(KT):
                    pe.wait_ge(lsq_made, l * 16 + n0 + o + 1)
                    mm(bank(7), CF[:, C_M1024:C_M1024 + P], T[o % 3][:, :], start=o == 0, stop=o == KT - 1)\
                        .then_inc(var_part, 1)

            def mean_step(l, which, o):
                pe.wait_ge(r_made, l * 40 + (32 if which else 0) + o + 1)
                m = mm(bank(6), CF[:, C_M1024:C_M1024 + P], R[:, o, :], start=o == 0, stop=o == KT - 1)
                if o == KT - 1:
                    m.then_inc(mean_made, 1)

            with pe.Fori(0, DEPTH) as l:
                def evacuated(by_dve=0, by_act=0):
                    if by_dve:
                        pe.wait_ge(dve_evac, l * 7 + by_dve)
                    if by_act:
                        pe.wait_ge(act_evac, l * 4 + by_act)

                def dense(n, t, b, wait_h=False):
                    w = lambda W_, k: W_[:, n % 2, k * 256 + t * P:k * 256 + t * P + P]
                    for k in range(KT):
                        if wait_h:
                            pe.wait_ge(hl_made, l * 16 + k + 1)
                        m = product(bank(b), [(w(WH, k), w(WL, k), HH[:, k, :], HL[:, k, :])], k == 0, k == KT - 1)
                    m.then_inc(tile_done, 1)

                def dense_tokens(n, lo, width, b, tokens):
                    for i, t in enumerate(tokens):
                        for k in range(KT):
                            cols = slice(k * 256 + lo, k * 256 + lo + width)
                            toks = slice(t * P, t * P + P)
                            out = bank(b, i * width, (i + 1) * width)
                            mm(out, HH[:, k, toks], WH[:, n % 2, cols], start=k == 0, stop=False)
                            mm(out, HL[:, k, toks], WH[:, n % 2, cols], start=False, stop=False)
                            m = mm(out, HH[:, k, toks], WL[:, n % 2, cols], start=False, stop=k == KT - 1)
                    m.then_inc(tile_done, 1)

                panel_made(0, l)
                dense(0, 0, 0, wait_h=True)
                dense(0, 1, 1)
                panel_made(1, l)
                dense(1, 0, 2)
                dense(1, 1, 3)
                pe.wait_ge(sq_made, l * 3 + 2)
                mm(bank(6), CF[:, C_M256:C_M256 + P], T[0][:, :], start=True, stop=False)
                mm(bank(6), CF[:, C_M256:C_M256 + P], T[1][:, :], start=False, stop=True).then_inc(ssq_made, 1)
                pe.wait_ge(sq_made, l * 3 + 3)
                mm(bank(7), CF[:, C_M128:C_M128 + P], T[2][:, :], start=True, stop=True).then_inc(ssq_made, 1)
                panel_made(2, l)
                dense(2, 0, 4)
                dense(2, 1, 5)
                panel_made(3, l)
                pe.wait_ge(cq_made, l * 2 + 1)
                dense(3, 0, 0)
                pe.wait_ge(cq_made, l * 2 + 2)
                dense(3, 1, 1)
                panel_made(4, l)
                evacuated(by_dve=1)
                dense(4, 0, 2)
                pe.wait_ge(krope_made, l * 4 + 4)
                dense(4, 1, 3)
                panel_made(5, l)
                evacuated(by_act=1)
                dense(5, 0, 4)
                evacuated(by_act=2)
                dense_tokens(5, P, P, 5, range(NT))
                panel_made(6, l)
                evacuated(by_dve=2)
                dense_tokens(6, 0, 2 * P, 0, (0, 1))
                evacuated(by_dve=3)
                dense_tokens(6, 0, 2 * P, 1, (2, 3))
                pe.wait_ge(ukv_in, l * 32 + 32)
                evacuated(by_dve=5)
                for t in range(NT):
                    mm(bank(4 + t), CKVN[:, t * P:(t + 1) * P], UV[:, :], start=True, stop=True)\
                        .then_inc(vbp_made, 1)
                evacuated(by_dve=7, by_act=4)
                pe.wait_ge(item_done, l * PER_LAYER + FIRST_ITEMS + POS["g", 7] + 1)
                modulation_sum(0)

                def scores_a(h):
                    rows = slice(HD * (h % 2), HD * (h % 2) + HD)
                    for j in reversed(range(NT)):
                        b = 4 * (h % 2) + j
                        if h == 0 and j == 0:
                            pe.wait_ge(mods_made, l * 3 + 2)
                        if h == 1 and j == NT - 1:
                            pe.wait_ge(vb_made, l * 4 + 4)
                        mm(bank(b, 0, CAUSAL[j]), KA[rows, h // 2, j * P:(j + 1) * P], QA[rows, h // 2, j * P:S],
                           start=True, stop=False)
                        mm(bank(b, 0, P), CB[:, 0:P], CB[:, P:2 * P], start=False, stop=True).then_inc(z_made, 1)

                def suffixes(h):
                    for i in reversed(range(NT)):
                        pe.wait_ge(sp_made, l * 16 + 4 * h + NT - i)
                        for j in range(i, NT):
                            c = C_TRI if j == i else C_NEG1
                            m = mm(bank(4 * (h % 2) + i, (j - i) * P, CAUSAL[i]), CF[:, c:c + P],
                                   W[h % 2][:, COFF[j]:COFF[j] + CAUSAL[j]], start=False, stop=True,
                                   skip_group_check=True)
                        m.then_inc(ex_made, 1)

                def values_a(h):
                    pe.wait_ge(w_made, l * 16 + 4 * h + 4)
                    row = HD * (h % 2)
                    for j in range(NT):
                        m = mm(PS[row:row + HD, 512 * (4 * (h % 2) + 3) + j * P:512 * (4 * (h % 2) + 4)],
                               VA[:, j, h * HD:(h + 1) * HD], W[2][:, COFF[j]:COFF[j] + CAUSAL[j]],
                               start=j == 0, stop=j == NT - 1)
                    m.then_inc(o_made, 1)

                scores_a(0)
                scores_a(1)
                for h in (0, 2):
                    suffixes(h)
                    suffixes(h + 1)
                    for k in (h, h + 1):
                        values_a(k)
                        if h == 0:
                            pe.wait_ge(ol_made, l * 16 + k + 1)
                            scores_a(k + 2)

                def key_product(pr):
                    mm(bank(7), UK[:, pr * P:(pr + 1) * P], CKVN[:, :], start=True, stop=True).then_inc(kp_made, 1)

                def query_product(h):
                    if h == 0:
                        panel_made(P_UQ, l)
                        pe.wait_ge(cql_made, l * 2 + 2)
                    w = lambda W_, k: W_[:, P_UQ % 2, k * 1024 + h * P:k * 1024 + h * P + P]
                    product(bank(7), [(w(WH, k), w(WL, k), CQH[:, k, :], CQL[:, k, :]) for k in range(2)])\
                        .then_inc(tile_done, 1)

                def scores_b(h):
                    pe.wait_ge(kn_made, l * 8 + h + 1)
                    pe.wait_ge(qn_made, l * 8 + h + 1)
                    pe.wait_ge(qr_made, l * 8 + h + 1)
                    if h >= 1:
                        pe.wait_ge(p_made, l * 32 + 4 * h)
                    for t in B_ORDER:
                        mm(b_scores(t), QB[0:QK_B, h % 4, t * P:(t + 1) * P], KB[0:QK_B, h % 4, 0:KEYS[t]],
                           start=True, stop=False)
                        mm(b_scores(t)[:, KEYS[t] - CHUNK:KEYS[t]], CB[0:1, 2 * P:3 * P], CB[0:1, 3 * P:3 * P + CHUNK],
                           start=False, stop=True).then_inc(s_made, 1)

                PT_BANK = ((3, 0), (4, 0), (5, 0), (4, 384))
                PT_AT = (0, 512, 896, 1152)

                def transposes_b(h):
                    pe.wait_ge(pn_made, l * 32 + 4 * h + 4)
                    for j in range(NT):
                        b, lo = PT_BANK[j]
                        for t in range(j, NT):
                            m = pe.transpose(bank(b, lo + (t - j) * P, lo + (t - j) * P + P),
                                             W[h % 2][:, KOFF[t] + j * P:KOFF[t] + j * P + P], ident)
                    m.then_inc(pt_made, 1)

                def values_b(h):
                    pe.wait_ge(pta_made, l * 20 + 2 * h + 2)
                    pe.wait_ge(ptd_made, l * 20 + 2 * h + 2)
                    if h >= 1:
                        pe.wait_ge(ol_made, l * 16 + 4 + h)
                    row = HD * (h % 2)
                    for j in range(NT):
                        m = mm(PS[row:row + HD, 512 * 6 + j * P:512 * 7], VB[:, j, h * HD:(h + 1) * HD],
                               W[2][:, PT_AT[j]:PT_AT[j] + CAUSAL[j]], start=j == 0, stop=j == NT - 1)
                    m.then_inc(o_made, 1)

                pe.wait_ge(item_done, l * PER_LAYER + FIRST_ITEMS + POS["g", 15] + 1)
                pe.wait_ge(ol_made, l * 16 + 4)
                modulation_sum(3)
                key_product(0)
                pe.wait_ge(kn_made, l * 8 + 2)
                query_product(0)
                scores_b(0)
                pe.wait_ge(mods_made, l * 3 + 3)
                for h in range(NH_B):
                    if h + 1 < NH_B:
                        if (h + 1) % 2 == 0:
                            key_product((h + 1) // 2)
                            pe.wait_ge(kn_made, l * 8 + h + 3)
                        query_product(h + 1)
                        scores_b(h + 1)
                    transposes_b(h)
                    values_b(h)
                pe.wait_ge(item_done, l * PER_LAYER + FIRST_ITEMS + POS["n", 7] + 1)
                modulation_sum(7)

                def scores_c(c):
                    if c == 0:
                        pe.wait_ge(p_made, l * 32 + 32)
                    if c >= 2:
                        pe.wait_ge(nmc_made, l * 4 + c - 1)
                    rows = slice(HD * (c // 2), HD * (c // 2) + HD)
                    for t in range(NT):
                        q = QC[rows, c % 2, t * P:(t + 1) * P]
                        at = 1024 * (c % 2) + 256 * t
                        if t == 0:
                            for k in range(2):
                                mm(PS[:, at + k * P:at + k * P + P], q, KC[rows, 0:P], start=True, stop=True)
                        else:
                            m = mm(PS[:, at:at + 2 * P], q, KC[rows, (t - 1) * P:(t + 1) * P], start=True, stop=True)
                    m.then_inc(sc_made, 1)

                def transposes_c(c):
                    wv = W[c % 2][:, 0:1024].rearrange("p (t k) -> p t k", t=NT)
                    pe.wait_ge(pnc_made, l * 16 + 4 * c + 4)
                    for j in range(NT):
                        for k in range(2):
                            if j + k < NT:
                                at = 2048 + 256 * j + k * P
                                m = pe.transpose(PS[:, at:at + P], wv[:, j + k, P * (1 - k):P * (1 - k) + P], ident)
                    m.then_inc(ptc_made, 1)

                def values_c(c):
                    pe.wait_ge(pta_made, l * 20 + 16 + c + 1)
                    pe.wait_ge(ptd_made, l * 20 + 16 + c + 1)
                    pe.wait_ge(ol_made, l * 16 + 12 + c)
                    row = HD * (c % 2)
                    kv = slice(HD * (c // 2), HD * (c // 2) + HD)
                    for t in range(NT):
                        out = PS[row:row + HD, 512 * 6 + t * P:512 * 6 + t * P + P]
                        m = mm(out, VC[:, t, kv], W[2][:, 256 * t:256 * t + P], start=True, stop=t == 0)
                        if t > 0:
                            m = mm(out, VC[:, t - 1, kv], W[2][:, 256 * (t - 1) + P:256 * t], start=False, stop=True)
                    m.then_inc(o_made, 1)

                scores_c(0)
                for c in range(NH_C):
                    if c + 1 < NH_C:
                        scores_c(c + 1)
                    transposes_c(c)
                    values_c(c)

                pe.wait_ge(oh_made, l * 16 + 16)
                pe.wait_ge(ol_made, l * 16 + 16)
                for n in range(P_OUT, P_FF):
                    panel_made(n, l)
                    for t in range(2):
                        o = 2 * (n - P_OUT) + t
                        if o >= 4:
                            pe.wait_ge(r_made, l * 40 + o - 3)
                        dense(n, t, o % 4)
                        if o >= 1:
                            mean_step(l, 0, o - 1)
                mean_step(l, 0, KT - 1)
                layer_norm_pe(l, 0, interleaved=True)

                with pe.Fori(0, QUARTERS) as q:
                    for j in range(8):
                        n = P_FF + j
                        panel_made(n, l, q)
                        for t in range(2):
                            u = 2 * j + t
                            if u < 4:
                                pe.wait_ge(r_made, l * 40 + q * 8 + 8 - 3 + u)
                            elif u < 12:
                                pe.wait_ge(relu_made, l * 32 + q * 8 + u - 3)
                            else:
                                pe.wait_ge(r_made, l * 40 + q * 8 + 8 + u - 11)
                            w = lambda W_, k: W_[:, n % 2, k * 256 + t * P:k * 256 + t * P + P]
                            for k in range(KT):
                                if u == 0:
                                    pe.wait_ge(hl_made, l * 16 + 8 + k + 1)
                                if u == 8:
                                    pe.wait_ge(fl_made, l * 32 + q * 8 + k + 1)
                                xh, xl = (HH, HL) if j < 4 else (FH, FL)
                                m = product(bank(u % 4), [(w(WH, k), w(WL, k), xh[:, k, :], xl[:, k, :])],
                                            k == 0, k == KT - 1)
                            m.then_inc(tile_done, 1)
                layer_norm_pe(l, 1)


def constants():
    cf = np.zeros((P, NCF), np.float32)
    k = np.arange(P)
    cf[:, C_ID:C_ID + P] = np.eye(P)
    cf[:, C_TRI:C_TRI + P] = -(k[:, None] >= k[None, :]).astype(np.float32)
    cf[:, C_NEG1:C_NEG1 + P] = -1.0
    cf[:, C_M1024:C_M1024 + P] = 1.0 / D
    cf[:, C_M256:C_M256 + P] = 1.0 / Q_LORA
    cf[:, C_M128:C_M128 + P] = 1.0 / KV_LORA
    freq = (np.float32(1.0) / (np.float32(10000.0) ** (np.arange(0, ROPE, 2, dtype=np.float32) / np.float32(ROPE))))
    cf[:, C_FREQ] = freq.astype(np.float32)[k % 16]
    cf[:, C_SIGN] = np.where((k % 32) < 16, -1.0, 1.0)
    cf[:, C_EPS] = LN_EPS
    cf[:, C_ONE] = 1.0
    cf[:, C_ALPHA] = ALPHA
    cb = np.zeros((P, 512), np.float32)
    cb[:, 0:P] = np.eye(P)
    cb[:, P:2 * P] = np.where(k[:, None] >= k[None, :], NEG, 0.0)
    cb[:, 2 * P:3 * P] = np.where(k[None, :] < CHUNK, NEG, 0.0)
    cb[:, 3 * P:] = 1.0
    col = np.arange(2 * P)
    lo = np.where(k < CHUNK, CHUNK, 2 * CHUNK)[:, None]
    maskc = np.where((col[None, :] >= lo) & (col[None, :] < lo + 2 * CHUNK), 0.0, FAR).astype(np.float32)
    return cf, cb, maskc


def panel(w):
    return w.reshape(KT, P, 256).transpose(1, 0, 2).reshape(P, ITEM)


def layer_items(a, l):
    w = a["w_in"][l]
    qa, ka, va, cq, ckv, kr, qc, kc, vc = np.split(w, np.cumsum([256, 256, 256, Q_LORA, KV_LORA, ROPE, 256, 128]), axis=1)
    half = ROPE // 2
    krs = np.concatenate([kr, kr[:, half:], kr[:, :half]], axis=1)
    qc = qc.reshape(D, 2, 2, HD).transpose(0, 2, 1, 3).reshape(D, 256)
    mats = [cq, np.concatenate([ckv, krs, krs], 1), qa, ka, qc, np.concatenate([kc, vc], 1), va]
    uq = a["w_uq"][l].reshape(Q_LORA, NH_B, QK_B)
    uq = np.concatenate([uq, uq[:, :, NOPE + half:], uq[:, :, NOPE:NOPE + half]], axis=2)
    out = [panel(m) for m in mats]
    out.append(uq.reshape(2, P, 1024).transpose(1, 0, 2).reshape(P, ITEM))
    out += [panel(a["w_out"][l][:, 256 * j:256 * j + 256]) for j in range(4)]
    for q in range(QUARTERS):
        out += [panel(a["w_ff1"][l][:, D * q + 256 * j:D * q + 256 * j + 256]) for j in range(4)]
        out += [panel(a["w_ff2"][l][D * q:D * q + D, 256 * j:256 * j + 256]) for j in range(4)]
    return out


def mod_item(a, l, i):
    third, k = divmod(i, KT)
    return a["ada_w"][l][k * P:(k + 1) * P, third * ITEM:(third + 1) * ITEM]


def column(v):
    return v.reshape(-1, P).T


def layout(a):
    panels = [layer_items(a, l) for l in range(DEPTH)]
    items = [mod_item(a, 0, i) for i in range(8)] + panels[0][:2]
    for l in range(DEPTH):
        nxt = (l + 1) % DEPTH
        for what in ORDER:
            if isinstance(what, tuple):
                items.append(mod_item(a, l, 8 + what[1]) if what[0] == "g" else mod_item(a, nxt, what[1]))
            else:
                items.append(panels[l][what] if what < PANELS else panels[nxt][what - PANELS])
    stream = np.stack(items)
    ukv = []
    vecs = np.zeros((P, DEPTH + 1, NVEC), np.float32)
    for l in range(DEPTH):
        w = a["w_ukv"][l].reshape(KV_LORA, NH_B, NOPE + HD)
        ukv.append(np.concatenate([w[:, :, :NOPE].reshape(P, 512), w[:, :, NOPE:].reshape(P, 512)], axis=1))
    for i in range(DEPTH + 1):
        l = i % DEPTH
        parts = [a[n][l] for n in ("ada_b", "q_norm_g", "kv_norm_g", "ln1_g", "ln1_b", "ln2_g", "ln2_b")]
        vecs[:, i, :V_SINK] = np.concatenate([column(v) for v in parts], axis=1)
        vecs[:, i, V_SINK:V_SINK + NH_C] = np.broadcast_to(a["sinks"][l], (P, NH_C))
    xT = a["x"][0].T.reshape(KT, P, S).transpose(1, 0, 2)
    return {"stream": stream, "ukv": np.stack(ukv), "x": xT, "vecs": vecs, "c": column(a["c"][0]),
            "pos": a["positions"], "posq": a["positions"][0].reshape(NT, P).T}


LINKS = {"act": 8, "dve": 125, "dve_q": 8}


def kernel(**inputs):
    import concourse.bacc as _bacc
    from concourse.bass_utils import run_bass_kernel_spmd as _run

    a = {k: np.asarray(v) for k, v in inputs.items()}
    data = layout(a)
    cf, cb, maskc = constants()
    import ml_dtypes
    data.update(cf=cf, cb=cb.astype(ml_dtypes.bfloat16), maskc=maskc)
    nc = _bacc.Bacc("TRN2", target_bir_lowering=False, num_devices=1)
    arrays, args = {}, []
    for name, v in data.items():
        v = np.ascontiguousarray(v)
        arrays[f"in_{name}"] = v
        args.append(nc.dram_tensor(f"in_{name}", v.shape, mybir.dt.from_np(v.dtype), kind="ExternalInput").ap())
    out = nc.dram_tensor("out_x", (P, KT, S), F32, kind="ExternalOutput").ap()
    build(nc, *args, out, LINKS)
    got = _run(nc, [arrays], core_ids=[0]).results[0]["out_x"]
    return np.ascontiguousarray(np.asarray(got).transpose(1, 0, 2).reshape(D, S).T)[None]
```

```python
from contextlib import ExitStack

import numpy as np
import concourse.bass as bass
from concourse import mybir

F32 = mybir.dt.float32
F32R = mybir.dt.float32r
BF16 = mybir.dt.bfloat16
I32 = mybir.dt.int32
ALU = mybir.AluOpType
ACT = mybir.ActivationFunctionType
AXX = mybir.AxisListType.X

P = 128
S = 512
D = 1024
KT = D // P
DEPTH = 2
NT = S // P
CHUNK = 64
NH_A, NH_B, NH_C, HD = 4, 8, 4, 64
NOPE, ROPE = 64, 32
QK_B = NOPE + ROPE
Q_LORA, KV_LORA = 256, 128
D_FF = 4 * D
QUARTERS = 4
ALPHA = float((2 * DEPTH) ** 0.25)
LN_EPS = 1e-5
NEG = -1e30
FAR = 1e34
SLOPES = [2.0 ** (-8.0 * (h + 1) / NH_C) for h in range(NH_C)]
ITEM = 2048
CAUSAL = [S - P * j for j in range(NT)]
COFF = [sum(CAUSAL[:j]) for j in range(NT)]
KEYS = [P * (t + 1) for t in range(NT)]
KOFF = [sum(KEYS[:t]) for t in range(NT)]

P_UQ, P_OUT, P_FF = 7, 8, 12
PANELS = P_FF + 8 * QUARTERS
ORDER = ([("g", 0), ("g", 1), 2, ("g", 2), 3, 4, ("g", 3), 5, ("g", 4), 6, ("g", 5), ("g", 6), 7, ("g", 7), 8,
          ("g", 8), ("g", 9), 9, 10, ("g", 10), ("g", 11), 11, ("g", 12), ("g", 13), 12, ("g", 14), ("g", 15)]
         + list(range(13, PANELS - 6))
         + [PANELS - 6, ("n", 0), PANELS - 5, ("n", 1), ("n", 2), PANELS - 4, ("n", 3), PANELS - 3, ("n", 4),
            PANELS - 2, ("n", 5), PANELS - 1, ("n", 6), PANELS, ("n", 7), PANELS + 1])
PER_LAYER = len(ORDER)
FIRST_ITEMS = 10
RAW = 4
POS = {what: i for i, what in enumerate(ORDER)}
assert PER_LAYER % RAW == 0 and PER_LAYER == 68
TILES = 14 + NH_B + KT + 16 * QUARTERS
T_UQ, T_OUT, T_FF = 14, 14 + NH_B, 14 + NH_B + KT

V_ADAB, V_QG, V_KVG, V_LN1G, V_LN1B, V_LN2G, V_LN2B, V_SINK, NVEC = 0, 48, 50, 51, 59, 67, 75, 83, 88
C_ID, C_TRI, C_NEG1, C_M1024, C_M256, C_M128, C_FREQ, C_SIGN, C_EPS, C_ONE, C_ALPHA = \
    0, 128, 256, 384, 512, 640, 768, 769, 770, 771, 772
NCF = 776
TWO_PI_PARTS = (6.28125, 0.0019350051879882812, 3.019916050561733e-07)


class Chain:

    def __init__(self, eng, sem):
        self.eng, self.sem, self.base, self.n = eng, sem, 0, 0

    def link(self, ins):
        self.n += 1
        ins.then_inc(self.sem, 1)
        self.eng.wait_ge(self.sem, self.base + self.n)


def build(nc, stream, ukv_d, x_d, vec_d, cT_d, pos_d, posq_d, cf_d, cb_d, maskc_d, out_d, links):
    ctx = ExitStack()
    with ctx:
        top = [(nc.sbuf_base + 31) // 32 * 32]

        def place(name, shape, dt, at=None):
            size = int(np.prod(shape[1:])) * (2 if dt == BF16 else 4)
            size = (size + 31) // 32 * 32
            if at is None:
                at = top[0]
                top[0] += size
            return nc.alloc_sbuf_tensor_at(name, shape, dt, offset=at), at + size

        def sb(name, shape, dt=F32):
            return place(name, shape, dt)[0]

        def sem(name):
            return ctx.enter_context(nc.semaphore(name))

        X = sb("X", [P, KT, S])
        HH = sb("HH", [P, KT, S], F32R)
        HL = sb("HL", [P, KT, S], F32R)
        raw = sb("raw", [P, RAW, ITEM])
        WH = sb("WH", [P, 2, ITEM], F32R)
        WL = sb("WL", [P, 2, ITEM], F32R)
        acc = sb("acc", [P, ITEM])
        UK = sb("UK", [P, 512])
        COS = sb("COS", [P, S])
        SIN = sb("SIN", [P, S])
        DIST = sb("DIST", [P, NT, 2 * P])
        CF = sb("CF", [P, NCF])
        CB = sb("CB", [P, 512], BF16)
        VEC = sb("VEC", [P, DEPTH + 1, NVEC])
        vec = sb("vec", [P, NVEC])
        modA = sb("modA", [P, 16])
        modB = sb("modB", [P, 32])
        g1p, g2p = sb("g1p", [P, 8]), sb("g2p", [P, 8])
        scp = sb("scp", [P, 8])
        gs1, bs1 = sb("gs1", [P, 8]), sb("bs1", [P, 8])
        gs2, bs2 = sb("gs2", [P, 8]), sb("bs2", [P, 8])
        cs = sb("cs", [P, KT])
        ce = sb("ce", [P, KT])
        mx = sb("mx", [P, 2, NT])
        nm = sb("nm", [P, 2, NT])
        den = sb("den", [P, 2, NT])
        esink = sb("esink", [P, 2, NT])
        rden = sb("rden", [P, 2, NT])
        CQH = sb("CQH", [P, 2, S], F32R)
        CQL = sb("CQL", [P, 2, S], F32R)
        shared = top[0]
        R = sb("R", [P, KT, S])
        FH = sb("FH", [P, KT, S], F32R)
        FL = sb("FL", [P, KT, S], F32R)
        end_shared = top[0]
        at = shared

        def over(name, shape, dt=F32):
            nonlocal at
            t, at = place(name, shape, dt, at)
            return t

        QB = over("QB", [P, 4, S])
        KB = over("KB", [P, 4, S])
        VB = over("VB", [P, NT, NH_B * HD])
        QA, KA = over("QA", [P, 2, S]), over("KA", [P, 2, S])
        VA = over("VA", [P, NT, NH_A * HD])
        QC, KC = over("QC", [P, 2, S]), over("KC", [P, S])
        VC = over("VC", [P, NT, 128])
        CKVN = over("CKVN", [P, S])
        UV = over("UV", [P, 512])
        assert at <= end_shared, (at, end_shared)
        work = top[0]
        W = [sb(f"W{i}", [P, 1280]) for i in range(3)]
        assert top[0] <= nc.sbuf_usable_end, (top[0], nc.sbuf_usable_end)
        at = work
        T = [over(f"T{i}", [P, S]) for i in range(7)]

        PS = ctx.enter_context(nc.psum_tensor("PS", [P, 8 * 512], F32))

        def bank(b, lo=0, hi=512):
            return PS[:, 512 * b + lo:512 * b + hi]

        raw_in = [sem(f"raw_in{i}") for i in range(RAW)]
        c_in = sem("c_in")
        small_in = sem("small_in")
        x_in = sem("x_in")
        ukv_in = sem("ukv_in")
        out_done = sem("out_done")
        item_done = sem("item_done")
        hi_made = sem("hi_made")
        tile_done = sem("tile_done")
        hh_made, hl_made = sem("hh_made"), sem("hl_made")
        x_made = sem("x_made")
        modsum = sem("modsum")
        mods_made = sem("mods_made")
        dchain, achain = sem("dchain"), sem("achain")
        silu_e = sem("silu_e")
        trig_in, trig_made = sem("trig_in"), sem("trig_made")
        silu_made = sem("silu_made")
        sq_made = sem("sq_made")
        ssq_made = sem("ssq_made")
        rs_exp = sem("rs_exp")
        cq_made, cqh_made, cql_made = sem("cq_made"), sem("cqh_made"), sem("cql_made")
        dve_evac, act_evac = sem("dve_evac"), sem("act_evac")
        vb_made = sem("vb_made")
        vbp_made = sem("vbp_made")
        vc_turned = sem("vc_turned")
        z_made, az_made, ln_made, sp_made = sem("z_made"), sem("az_made"), sem("ln_made"), sem("sp_made")
        ex_made, w_made = sem("ex_made"), sem("w_made")
        o_made, oh_made, ol_made = sem("o_made"), sem("oh_made"), sem("ol_made")
        kp_made, kn_made, krope_made = sem("kp_made"), sem("kn_made"), sem("krope_made")
        qn_made, qr_made = sem("qn_made"), sem("qr_made")
        s_made, nm_made, p_made, pn_made = sem("s_made"), sem("nm_made"), sem("p_made"), sem("pn_made")
        pt_made, ptc_made, pta_made, ptd_made = sem("pt_made"), sem("ptc_made"), sem("pta_made"), sem("ptd_made")
        sc_made, nmc_made, pc_made, pnc_made = sem("sc_made"), sem("nmc_made"), sem("pc_made"), sem("pnc_made")
        rden_made = sem("rden_made")
        r_init = sem("r_init")
        r_made = sem("r_made")
        rsum_made = sem("rsum_made")
        sqp_made = sem("sqp_made")
        mean_made, dif_made, lsq_made, var_made = sem("mean_made"), sem("dif_made"), sem("lsq_made"), sem("var_made")
        var_exp = sem("var_exp")
        u_made, xg_made = sem("u_made"), sem("xg_made")
        relu_made, fh_made, fl_made, ft_read = sem("relu_made"), sem("fh_made"), sem("fl_made"), sem("ft_read")

        ident = CF[:, C_ID:C_ID + P]
        block = ctx.enter_context(nc.Block())

        def raw_count(i, l=None, q=0):
            n = 16 * ((FIRST_ITEMS + i) // RAW + 1)
            return n if l is None else l * (16 * PER_LAYER // RAW) + q * (16 * 8 // RAW) + n

        def raw_slot(i):
            return (FIRST_ITEMS + i) % RAW

        B_ORDER = (0, 2, 1, 3)
        UQ_BANK = (7, 4) + (7,) * (NH_B - 2)
        SQUARE_AT = (0, 1, 2, 3, 5, 6, 1, 3)
        PAIR_FREES = {6: 1, 7: 2}
        OUT_BANK = (7, 1, 2, 3, 0, 1, 2, 3)

        def b_scores(t):
            b, lo = ((1, 384), (2, 0), (1, 0), (0, 0))[t]
            return bank(b, lo, lo + KEYS[t])

        @block.sync
        def _(sp):
            sp.dma_start(cs[:, :], cT_d).then_inc(c_in, 16)
            for n in range(RAW):
                sp.dma_start(raw[:, n, :], stream[n, :, :]).then_inc(raw_in[n], 16)
            sp.dma_start(VEC[:, :, :], vec_d).then_inc(small_in, 16)
            sp.dma_start(CF[:, :], cf_d).then_inc(small_in, 16)
            sp.dma_start(CB[:, :], cb_d).then_inc(small_in, 16)
            sp.dma_start(T[0][:, :].bitcast(I32), pos_d.to_broadcast([P, S])).then_inc(small_in, 16)
            sp.dma_start(mx[:, 0, :].bitcast(I32), posq_d).then_inc(small_in, 16)
            sp.dma_start(T[3][:, 0:2 * P], maskc_d).then_inc(small_in, 16)
            total = FIRST_ITEMS + DEPTH * PER_LAYER
            for n in range(RAW, 2 * RAW):
                sp.wait_ge(item_done, n - RAW + 1)
                sp.dma_start(raw[:, n % RAW, :], stream[n, :, :]).then_inc(raw_in[n % RAW], 16)
            sp.dma_start(X[:, :, :], x_d).then_inc(x_in, 16)
            rest = (total - RAW) % RAW
            with sp.Fori(1, (total - rest) // RAW - 1) as g:
                for k in range(RAW):
                    sp.wait_ge(item_done, g * RAW + k + 1)
                    sp.dma_start(raw[:, k, :], stream[bass.ds(g * RAW + RAW + k, 1), :, :].rearrange("a p n -> (a p) n"))\
                      .then_inc(raw_in[k], 16)
            for n in range(total - rest, total):
                sp.wait_ge(item_done, n - RAW + 1)
                sp.dma_start(raw[:, n % RAW, :], stream[n, :, :]).then_inc(raw_in[n % RAW], 16)
            for o in range(0, KT, 2):
                sp.wait_ge(x_made, 16 * DEPTH - KT + o + 2)
                sp.dma_start(out_d[:, o:o + 2, :], X[:, o:o + 2, :]).then_inc(out_done, 16)
            sp.wait_ge(out_done, 16 * (KT // 2))

        @block.gpsimd
        def _(pool):
            alpha = CF[:, C_ALPHA:C_ALPHA + 1].to_broadcast([P, S])
            add = ALU.add

            def residual_sum(l, which):
                made = 8 * QUARTERS if which else 0
                n = l * 12 + 6 * which
                pool.wait_ge(r_made, l * 40 + made + 2)
                pool.tensor_tensor(T[5][:, :], R[:, 0, :], R[:, 1, :], add).then_inc(rsum_made, 1)
                for o in range(2, KT - 1):
                    pool.wait_ge(r_made, l * 40 + made + o + 1)
                    pool.wait_ge(rsum_made, n + o - 1)
                    pool.tensor_tensor(T[5][:, :], T[5][:, :], R[:, o, :], add).then_inc(rsum_made, 1)

            def square_pairs(l, which):
                for k in range(2):
                    pool.wait_ge(lsq_made, l * 16 + 8 * which + 2 * k + 2)
                    a, b = T[2 * k], T[2 * k + 1]
                    pool.tensor_tensor(a[:, :], a[:, :], b[:, :], add).then_inc(sqp_made, 1)

            pool.wait_ge(small_in, 16 * 6)
            with pool.Fori(0, DEPTH) as l:
                for h in range(NH_B):
                    pool.wait_ge(rden_made, l * 12 + h + 1)
                    for t in range(NT):
                        w = W[h % 2][:, KOFF[t]:KOFF[t] + KEYS[t]]
                        pool.tensor_tensor(w, w, rden[:, h % 2, t:t + 1].to_broadcast([P, KEYS[t]]), ALU.mult)\
                            .then_inc(pn_made, 1)
                for c in range(NH_C):
                    pool.wait_ge(rden_made, l * 12 + NH_B + c + 1)
                    for t in range(NT):
                        w = W[c % 2][:, 256 * t:256 * t + 256]
                        pool.tensor_tensor(w, w, rden[:, c % 2, t:t + 1].to_broadcast([P, 256]), ALU.mult)\
                            .then_inc(pnc_made, 1)
                pool.wait_ge(o_made, l * 16 + 16)
                pool.wait_ge(oh_made, l * 16 + 16)
                pool.wait_ge(ol_made, l * 16 + 16)
                for o in range(KT):
                    pool.tensor_tensor(R[:, o, :], X[:, o, :], alpha, ALU.mult).then_inc(r_init, 1)
                residual_sum(l, 0)
                square_pairs(l, 0)
                for o in range(KT):
                    pool.wait_ge(x_made, l * 16 + o + 1)
                    pool.tensor_tensor(R[:, o, :], X[:, o, :], alpha, ALU.mult).then_inc(r_init, 1)
                residual_sum(l, 1)
                square_pairs(l, 1)

        @block.scalar
        def _(act):
            chain = Chain(act, achain)
            link = chain.link
            eps = CF[:, C_EPS:C_EPS + 1]

            def high(n, l=None, q=0):
                i = POS.get(n)
                if l is None:
                    i = n - 2
                    act.wait_ge(raw_in[raw_slot(i)], raw_count(i))
                else:
                    if isinstance(q, int):
                        i, iq = POS[n + 8 * q], 0
                    else:
                        iq = q
                    act.wait_ge(raw_in[raw_slot(i)], raw_count(i, l, iq))
                    free = 2 * (n - 1) if n < 9 else T_OUT + 2 * (n - 9) if n > 9 else T_OUT
                    act.wait_ge(tile_done, l * TILES + q * 16 + free)
                act.activation(WH[:, n % 2, :], raw[:, raw_slot(i), :], ACT.Copy).then_inc(hi_made, 1)

            def h_high(o, src, g, b, inc=hh_made):
                act.activation(HH[:, o, :], src, ACT.Identity, scale=g[:, o:o + 1], bias=b[:, o:o + 1])\
                   .then_inc(inc, 1)

            act.wait_ge(c_in, 16)
            act.activation(ce[:, :], cs[:, :], ACT.Exp, scale=-1.0).then_inc(silu_e, 1)
            high(0)
            high(1)
            act.wait_ge(x_in, 16)
            act.wait_ge(mods_made, 1)
            for o in range(KT):
                h_high(o, X[:, o, :], gs2, bs2)
            act.wait_ge(small_in, 16 * 6)
            act.wait_ge(trig_in, 1)
            act.activation(SIN[:, :], T[1][:, :], ACT.Sin).then_inc(trig_made, 1)
            act.wait_ge(trig_in, 2)
            act.activation(COS[:, :], T[2][:, :], ACT.Sin).then_inc(trig_made, 1)
            act.wait_ge(trig_made, 2)
            act.preload_act_table_set("natural_log_exp_and_others")

            def layer_norm_act(l, which):
                n0 = 8 * which
                for o in range(KT):
                    act.wait_ge(dif_made, l * 16 + n0 + o + 1)
                    if o in PAIR_FREES:
                        act.wait_ge(sqp_made, l * 4 + 2 * which + PAIR_FREES[o])
                    act.activation(T[SQUARE_AT[o]][:, :], R[:, o, :], ACT.Square).then_inc(lsq_made, 1)
                act.wait_ge(var_made, l * 2 + which + 1)
                link(act.activation(T[3][:, :], bank(7), ACT.Ln, bias=eps))
                act.activation(T[4][:, :], T[3][:, :], ACT.Exp, scale=-0.5).then_inc(var_exp, 1)
                b, vb = ((bs1, V_LN1B), (bs2, V_LN2B))[which]
                for o in range(KT):
                    act.wait_ge(u_made, l * 16 + n0 + o + 1)
                    act.activation(HH[:, o, :], T[5 + o % 2][:, :], ACT.Identity, bias=b[:, o:o + 1]).then_inc(hh_made, 1)
                for o in range(KT):
                    act.wait_ge(xg_made, l * 16 + n0 + o + 1)
                    act.activation(X[:, o, :], R[:, o, :], ACT.Identity, bias=vec[:, vb + o:vb + o + 1])\
                       .then_inc(x_made, 1)

            n_start = chain.n
            with act.Fori(0, DEPTH) as l:
                chain.base, chain.n = n_start + l * links["act"], 0

                def tile(n):
                    act.wait_ge(tile_done, l * TILES + n)

                act.wait_ge(hl_made, l * 16 + 8)
                ukv = ukv_d[bass.ds(l, 1), :, :].rearrange("a p n -> (a p) n")
                act.dma_start(UK[:, :], ukv[:, 0:512]).then_inc(ukv_in, 16)
                act.dma_start(UV[:, :], ukv[:, 512:1024]).then_inc(ukv_in, 16)
                tile(1)
                act.activation(T[0][:, :], bank(0), ACT.Square).then_inc(sq_made, 1)
                tile(2)
                act.activation(T[1][:, :], bank(1), ACT.Square).then_inc(sq_made, 1)
                high(2, l)
                tile(3)
                act.activation(T[2][:, :], bank(2), ACT.Square).then_inc(sq_made, 1)
                high(3, l)
                act.wait_ge(ssq_made, l * 2 + 1)
                link(act.activation(T[3][:, :], bank(6), ACT.Ln, bias=eps))
                act.activation(T[4][:, :], T[3][:, :], ACT.Exp, scale=-0.5).then_inc(rs_exp, 1)
                tile(5)
                act.activation(QA[:, 0, :], bank(4), ACT.Copy, scale=HD ** -0.5).then_inc(act_evac, 1)
                for k in range(2):
                    act.wait_ge(cq_made, l * 2 + k + 1)
                    act.activation(CQH[:, k, :], T[k][:, :], ACT.Copy).then_inc(cqh_made, 1)
                tile(6)
                act.activation(QA[:, 1, :], bank(5), ACT.Copy, scale=HD ** -0.5).then_inc(act_evac, 1)
                high(4, l)
                act.wait_ge(ssq_made, l * 2 + 2)
                link(act.activation(T[5][:, :], bank(7), ACT.Ln, bias=eps))
                act.activation(T[6][:, :], T[5][:, :], ACT.Exp, scale=-0.5).then_inc(rs_exp, 1)
                high(5, l)

                def soft(h):
                    for j in reversed(range(NT)):
                        w = W[0][:, COFF[j]:COFF[j] + CAUSAL[j]]
                        act.wait_ge(az_made, l * 16 + 4 * h + NT - j)
                        e = act.activation(w, w, ACT.Exp, scale=-1.0)
                    link(e)
                    for j in reversed(range(NT)):
                        w = W[0][:, COFF[j]:COFF[j] + CAUSAL[j]]
                        act.activation(w, w, ACT.Ln, bias=CF[:, C_ONE:C_ONE + 1]).then_inc(ln_made, 1)

                def weights(h):
                    if h >= 1:
                        act.wait_ge(o_made, l * 16 + h)
                    for i in reversed(range(NT)):
                        act.wait_ge(ex_made, l * 16 + 4 * h + NT - i)
                        act.activation(W[2][:, COFF[i]:COFF[i] + CAUSAL[i]],
                                       bank(i, 0, CAUSAL[i]), ACT.Exp).then_inc(w_made, 1)

                def mixed_high(u, b, row, tl):
                    act.wait_ge(o_made, l * 16 + u + 1)
                    act.activation(HH[row:row + HD, tl, :], PS[row:row + HD, 512 * b:512 * b + 512], ACT.Copy)\
                       .then_inc(oh_made, 1)

                def query_window(k):
                    tile(11 + k)
                    act.activation(QC[:, k, :], bank(4 + k), ACT.Copy, scale=HD ** -0.5).then_inc(act_evac, 1)

                def key_nope(pr):
                    act.wait_ge(kp_made, l * 4 + pr + 1)
                    for k in range(2):
                        if pr >= 2:
                            act.wait_ge(s_made, l * 32 + 4 * (2 * pr + k - 3))
                        act.activation(KB[0:NOPE, (2 * pr + k) % 4, :],
                                       PS[NOPE * k:NOPE * (k + 1), 512 * 7:512 * 8], ACT.Copy).then_inc(kn_made, 1)

                def query_nope(h):
                    tile(T_UQ + h + 1)
                    act.activation(QB[0:NOPE, h % 4, :], PS[0:NOPE, 512 * UQ_BANK[h]:512 * UQ_BANK[h] + 512], ACT.Copy).then_inc(qn_made, 1)

                def exps_b(h):
                    act.wait_ge(nm_made, l * 8 + h + 1)
                    for t in range(NT):
                        act.activation(W[h % 2][:, KOFF[t]:KOFF[t] + KEYS[t]], b_scores(t), ACT.Exp,
                                       bias=nm[:, h % 2, t:t + 1], scale=QK_B ** -0.5,
                                       accum_out=den[:, h % 2, t:t + 1]).then_inc(p_made, 1)

                def exps_c(c):
                    act.wait_ge(nmc_made, l * 4 + c + 1)
                    wv = W[c % 2][:, 0:1024].rearrange("p (t k) -> p t k", t=NT)
                    for t in range(NT):
                        act.activation(wv[:, t, :], wv[:, t, :], ACT.Exp, bias=nm[:, c % 2, t:t + 1],
                                       accum_out=den[:, c % 2, t:t + 1]).then_inc(pc_made, 1)
                    act.activation(esink[:, c % 2, :], nm[:, c % 2, :], ACT.Exp,
                                   bias=vec[:, V_SINK + c:V_SINK + c + 1]).then_inc(pc_made, 1)

                def latent_values(t):
                    act.wait_ge(vbp_made, l * 4 + t + 1)
                    act.activation(VB[:, t, :], bank(4 + t), ACT.Copy).then_inc(vb_made, 1)

                high(6, l)
                soft(0)
                query_window(0)
                weights(0)
                query_window(1)
                high(7, l)
                soft(1)
                weights(1)
                high(8, l)
                soft(2)
                mixed_high(0, 6, 0, 0)
                mixed_high(1, 6, HD, 0)
                latent_values(0)
                weights(2)
                key_nope(0)
                latent_values(1)
                soft(3)
                mixed_high(2, 6, 0, 1)
                query_nope(0)
                weights(3)
                query_nope(1)
                mixed_high(3, 6, HD, 1)
                exps_b(0)
                query_nope(2)
                for h in range(NH_B):
                    if h % 2 == 0 and h + 2 < NH_B:
                        key_nope((h + 2) // 2)
                    if h + 1 < NH_B:
                        exps_b(h + 1)
                    if h >= 1:
                        mixed_high(3 + h, 6, HD * ((h - 1) % 2), 2 + (h - 1) // 2)
                    act.wait_ge(pt_made, l * 8 + h + 1)
                    act.activation(W[2][:, 0:512], bank(3), ACT.Copy).then_inc(pta_made, 1)
                    act.activation(W[2][:, 896:1152], bank(5, 0, 256), ACT.Copy).then_inc(pta_made, 1)
                    if h + 3 < NH_B:
                        query_nope(h + 3)
                exps_c(0)
                mixed_high(11, 6, HD, 5)
                exps_c(1)
                high(9, l)
                for c in range(NH_C):
                    act.wait_ge(ptc_made, l * 4 + c + 1)
                    act.activation(W[2][:, 0:512], bank(4), ACT.Copy).then_inc(pta_made, 1)
                    if c + 2 < NH_C:
                        exps_c(c + 2)
                    mixed_high(12 + c, 6, HD * (c % 2), 6 + c // 2)

                for n in range(P_OUT, P_FF):
                    high(n + 2, l)
                layer_norm_act(l, 0)

                def quarter(q):
                    for j in range(8):
                        n = P_FF + j
                        if j < 4:
                            for t in range(2):
                                u = 2 * j + t
                                act.wait_ge(tile_done, l * TILES + q * 16 + (T_FF + u + 1))
                                if u >= 2:
                                    act.wait_ge(fl_made, l * 32 + q * 8 + (u - 1))
                                act.activation(T[u % 2][:, :], bank(u % 4), ACT.Relu).then_inc(relu_made, 1)
                                act.wait_ge(relu_made, l * 32 + q * 8 + (u + 1))
                                act.activation(FH[:, u, :], T[u % 2][:, :], ACT.Square).then_inc(fh_made, 1)
                        high(n + 2, l, q)

                with act.Fori(0, QUARTERS - 1) as q:
                    quarter(q)
                quarter(QUARTERS - 1)
                layer_norm_act(l, 1)
                assert chain.n == links["act"], ("act", chain.n)

        @block.vector
        def _(dve):
            chain = Chain(dve, dchain)
            link = chain.link
            tt, ts, stt = dve.tensor_tensor, dve.tensor_scalar, dve.scalar_tensor_tensor

            def magnitude(out, x):
                return ts(out.bitcast(I32), x.bitcast(I32), 0x7fffffff, None, ALU.bitwise_and)

            def low(n, l=None, q=0):
                i = n - 2 if l is None else POS[n + 8 * q] if isinstance(q, int) else POS[n]
                if l is None:
                    dve.wait_ge(hi_made, n + 1)
                else:
                    dve.wait_ge(hi_made, l * PANELS + q * 8 + n + 1)
                tt(WL[:, n % 2, :], raw[:, raw_slot(i), :], WH[:, n % 2, :].bitcast(F32), ALU.subtract)\
                    .then_inc(item_done, 1)

            def modulate(i, kt, l=None):
                if l is None:
                    dve.wait_ge(raw_in[raw_slot(i)], raw_count(i))
                else:
                    dve.wait_ge(raw_in[raw_slot(i)], raw_count(i, l))
                src = raw[:, raw_slot(i), :]
                if kt == 0:
                    ts(acc[:, :], src, cs[:, 0:1], None, ALU.mult).then_inc(item_done, 1)
                else:
                    if l is None:
                        dve.wait_ge(item_done, i + FIRST_ITEMS)
                    else:
                        dve.wait_ge(item_done, l * PER_LAYER + (i + FIRST_ITEMS))
                    stt(acc[:, :], src, cs[:, kt:kt + 1], acc[:, :], ALU.mult, ALU.add).then_inc(item_done, 1)

            def h_low(o, src, g, b, n):
                t = T[5 + o % 2]
                link(ts(t[:, :], src, g[:, o:o + 1], b[:, o:o + 1], ALU.mult, ALU.add))
                dve.wait_ge(hh_made, n)
                tt(HL[:, o, :], t[:, :], HH[:, o, :].bitcast(F32), ALU.subtract).then_inc(hl_made, 1)

            dve.wait_ge(silu_e, 1)
            link(ts(ce[:, :], ce[:, :], 1.0, None, ALU.add))
            link(dve.reciprocal(ce[:, :], ce[:, :]))
            link(tt(cs[:, :], cs[:, :], ce[:, :], ALU.mult))
            for kt in range(KT):
                modulate(kt - FIRST_ITEMS, kt)
            low(0)
            low(1)
            dve.wait_ge(small_in, 16 * 6)
            link(dve.tensor_copy(vec[:, :], VEC[:, 0, :]))
            dve.wait_ge(modsum, 1)
            link(tt(modA[:, :], bank(4, 0, 16), vec[:, 0:16], ALU.add))
            link(dve.tensor_copy(bs2[:, :], modA[:, 0:8]))
            ts(gs2[:, :], modA[:, 8:16], 1.0, None, ALU.add).then_inc(mods_made, 1)
            dve.wait_ge(mods_made, 1)
            dve.wait_ge(x_in, 16)
            for o in range(KT):
                h_low(o, X[:, o, :], gs2, bs2, o + 1)
            magic = 12582912.0
            link(dve.tensor_copy(T[4][:, :], T[0][:, :].bitcast(I32)))
            link(dve.tensor_copy(mx[:, 1, :], mx[:, 0, :].bitcast(I32)))
            for t in range(NT):
                lo = P * max(t - 1, 0)
                dst = DIST[:, t, P:2 * P] if t == 0 else DIST[:, t, :]
                n = P if t == 0 else 2 * P
                link(ts(dst, T[4][:, lo:lo + n], mx[:, 1, t:t + 1], None, ALU.subtract))
                link(magnitude(dst, dst))
                link(tt(dst, dst, T[3][:, 2 * P - n:2 * P], ALU.add))
            link(dve.memset(DIST[:, 0, 0:P], FAR))
            link(ts(T[5][:, :], T[4][:, :], CF[:, C_FREQ:C_FREQ + 1], None, ALU.mult))
            for k, quarter_turn in enumerate((0.0, 0.25)):
                link(ts(T[0][:, :], T[5][:, :], float(1 / (2 * np.pi)), quarter_turn, ALU.mult, ALU.add))
                link(ts(T[0][:, :], T[0][:, :], magic, None, ALU.add))
                link(ts(T[0][:, :], T[0][:, :], magic, None, ALU.subtract))
                r = T[1 + k]
                link(stt(r[:, :], T[0][:, :], -TWO_PI_PARTS[0], T[5][:, :], ALU.mult, ALU.add))
                link(stt(r[:, :], T[0][:, :], -TWO_PI_PARTS[1], r[:, :], ALU.mult, ALU.add))
                link(stt(r[:, :], T[0][:, :], -TWO_PI_PARTS[2], r[:, :], ALU.mult, ALU.add))
                if k:
                    link(ts(r[:, :], r[:, :], float(np.pi / 2), None, ALU.add))
                ts(r[:, :], r[:, :], 3.1415925, -3.1415925, ALU.min, ALU.max).then_inc(trig_in, 1)
            dve.wait_ge(trig_made, 2)
            link(ts(SIN[:, :], SIN[:, :], CF[:, C_SIGN:C_SIGN + 1], None, ALU.mult))

            def second_mods(l):
                dve.wait_ge(modsum, l * 3 + 3)
                tt(modB[:, 16:32], bank(4, 0, 16), vec[:, 32:48], ALU.add).then_inc(mods_made, 1)
                dve.wait_ge(mods_made, l * 3 + 3)
                link(ts(scp[:, :], modB[:, 16:24], 1.0, None, ALU.add))
                link(ts(g2p[:, :], modB[:, 24:32], 1.0, None, ALU.add))
                link(tt(gs1[:, :], vec[:, V_LN1G:V_LN1G + 8], scp[:, :], ALU.mult))
                link(tt(bs1[:, :], vec[:, V_LN1B:V_LN1B + 8], scp[:, :], ALU.mult))
                link(tt(bs1[:, :], bs1[:, :], modB[:, 8:16], ALU.add))

            def next_mods(l):
                dve.wait_ge(modsum, l * 3 + 4)
                tt(modA[:, :], bank(4, 0, 16), VEC[:, bass.ds(l + 1, 1), 0:16].rearrange("p a n -> p (a n)"), ALU.add)\
                    .then_inc(mods_made, 1)
                dve.wait_ge(mods_made, l * 3 + 4)
                link(ts(scp[:, :], modA[:, 8:16], 1.0, None, ALU.add))
                link(tt(gs2[:, :], vec[:, V_LN2G:V_LN2G + 8], scp[:, :], ALU.mult))
                link(tt(bs2[:, :], vec[:, V_LN2B:V_LN2B + 8], scp[:, :], ALU.mult))
                link(tt(bs2[:, :], bs2[:, :], modA[:, 0:8], ALU.add))

            def layer_norm_dve(l, which):
                n0 = 8 * which
                dve.wait_ge(mean_made, l * 2 + which + 1)
                for o in range(KT):
                    tt(R[:, o, :], R[:, o, :], bank(6), ALU.subtract).then_inc(dif_made, 1)
                if which == 0:
                    second_mods(l)
                    low(P_FF + 1, l)
                else:
                    next_mods(l)
                    low(P_FF + 9, l, QUARTERS - 1)
                dve.wait_ge(var_exp, l * 2 + which + 1)
                link(tt(T[3][:, :], T[4][:, :], T[4][:, :], ALU.mult))
                link(stt(T[3][:, :], bank(7), LN_EPS, T[3][:, :], ALU.add, ALU.mult))
                link(ts(T[3][:, :], T[3][:, :], -0.5, 1.5, ALU.mult, ALU.add))
                link(tt(T[4][:, :], T[3][:, :], T[4][:, :], ALU.mult))
                g, b, vg = ((gs1, bs1, V_LN1G), (gs2, bs2, V_LN2G))[which]

                def scaled(o):
                    stt(T[5 + o % 2][:, :], R[:, o, :], g[:, o:o + 1], T[4][:, :], ALU.mult, ALU.mult)\
                        .then_inc(u_made, 1)

                scaled(0)
                for o in range(KT):
                    if o + 1 < KT:
                        if o >= 1:
                            dve.wait_ge(hl_made, l * 16 + 8 + n0 + o)
                        scaled(o + 1)
                    dve.wait_ge(u_made, l * 16 + n0 + o + 1)
                    dve.wait_ge(hh_made, l * 16 + 8 + n0 + o + 1)
                    stt(HL[:, o, :], T[5 + o % 2][:, :], b[:, o:o + 1], HH[:, o, :].bitcast(F32), ALU.add, ALU.subtract)\
                        .then_inc(hl_made, 1)
                for o in range(KT):
                    stt(R[:, o, :], R[:, o, :], vec[:, vg + o:vg + o + 1], T[4][:, :], ALU.mult, ALU.mult)\
                        .then_inc(xg_made, 1)

            def rms_factor(l, k, y, t, b):
                dve.wait_ge(rs_exp, l * 2 + k + 1)
                link(tt(t[:, :], y[:, :], y[:, :], ALU.mult))
                link(stt(t[:, :], bank(b), LN_EPS, t[:, :], ALU.add, ALU.mult))
                link(ts(t[:, :], t[:, :], -0.5, 1.5, ALU.mult, ALU.add))
                link(tt(y[:, :], t[:, :], y[:, :], ALU.mult))

            n_start = chain.n
            with dve.Fori(0, DEPTH) as l:
                chain.base, chain.n = n_start + l * links["dve"], 0

                def tile(n):
                    dve.wait_ge(tile_done, l * TILES + n)

                def own(i):
                    modulate(POS["g", i], i % KT, l)

                def following(i):
                    modulate(POS["n", i], i, l)

                def absolute(h):
                    for j in reversed(range(NT)):
                        dve.wait_ge(z_made, l * 16 + 4 * h + NT - j)
                        magnitude(W[0][:, COFF[j]:COFF[j] + CAUSAL[j]], bank(j, 0, CAUSAL[j]))\
                            .then_inc(az_made, 1)

                def softplus(h):
                    for j in reversed(range(NT)):
                        dve.wait_ge(ln_made, l * 16 + 4 * h + NT - j)
                        w = W[0][:, COFF[j]:COFF[j] + CAUSAL[j]]
                        stt(w, bank(j, 0, CAUSAL[j]), 0.0, w, ALU.max, ALU.add).then_inc(sp_made, 1)

                def mixed_low(u, row, tl):
                    dve.wait_ge(oh_made, l * 16 + u + 1)
                    tt(HL[row:row + HD, tl, :], PS[row:row + HD, 512 * 6:512 * 7],
                       HH[row:row + HD, tl, :].bitcast(F32), ALU.subtract).then_inc(ol_made, 1)

                def rope_tmp(k):
                    return QA[NOPE:QK_B, k, :]

                def query_rope(h):
                    b = 512 * UQ_BANK[h]
                    if h >= 1:
                        dve.wait_ge(qr_made, l * 8 + h)
                    tile(T_UQ + h + 1)
                    link(tt(rope_tmp(0), PS[NOPE:QK_B, b:b + 512], COS[NOPE:QK_B, :], ALU.mult))
                    link(tt(rope_tmp(1), PS[QK_B:P, b:b + 512], SIN[QK_B:P, :], ALU.mult))
                    tt(QB[NOPE:QK_B, h % 4, :], rope_tmp(0), rope_tmp(1), ALU.add).then_inc(qr_made, 1)

                own(0)
                own(1)
                low(2, l)
                own(2)
                low(3, l)
                tile(4)
                link(tt(KA[NOPE:QK_B, 0, :], PS[NOPE:QK_B, 512 * 3:512 * 4], COS[NOPE:QK_B, :], ALU.mult))
                link(tt(KA[NOPE:QK_B, 1, :], PS[QK_B:P, 512 * 3:512 * 4], SIN[QK_B:P, :], ALU.mult))
                for k in range(4):
                    tt(KB[NOPE:QK_B, k, :], KA[NOPE:QK_B, 0, :], KA[NOPE:QK_B, 1, :], ALU.add)\
                        .then_inc(krope_made, 1)
                rms_factor(l, 0, T[4], T[3], 6)
                for k in range(2):
                    stt(T[k][:, :], bank(k), vec[:, V_QG + k:V_QG + k + 1], T[4][:, :], ALU.mult, ALU.mult)\
                        .then_inc(cq_made, 1)
                for k in range(2):
                    dve.wait_ge(cqh_made, l * 2 + k + 1)
                    tt(CQL[:, k, :], T[k][:, :], CQH[:, k, :].bitcast(F32), ALU.subtract).then_inc(cql_made, 1)
                low(4, l)
                rms_factor(l, 1, T[6], T[5], 7)
                stt(CKVN[:, :], bank(2), vec[:, V_KVG:V_KVG + 1], T[6][:, :], ALU.mult, ALU.mult)\
                    .then_inc(dve_evac, 1)
                own(3)
                for k in range(2):
                    tile(7 + k)
                    dve.tensor_copy(KA[:, k, :], bank(k)).then_inc(dve_evac, 1)
                low(5, l)
                own(4)
                for k in range(2):
                    tile(9 + k)
                    dve.tensor_copy(VA[:, 2 * k:2 * k + 2, :], bank(2 + k).rearrange("p (t n) -> p t n", t=2))\
                        .then_inc(dve_evac, 1)

                absolute(0)
                low(6, l)
                softplus(0)
                own(5)
                own(6)
                absolute(1)
                low(7, l)
                softplus(1)
                tile(13)
                dve.tensor_copy(KC[:, :], bank(4)).then_inc(dve_evac, 1)
                own(7)
                tile(14)
                dve.tensor_copy(T[3][:, :], bank(5)).then_inc(dve_evac, 1)
                absolute(2)
                low(8, l)
                softplus(2)
                dve.wait_ge(modsum, l * 3 + 2)
                tt(modB[:, 0:16], bank(7, 0, 16), vec[:, 16:32], ALU.add).then_inc(mods_made, 1)
                dve.wait_ge(mods_made, l * 3 + 2)
                link(ts(g1p[:, :], modB[:, 0:8], 1.0, None, ALU.add))
                dve.wait_ge(vc_turned, l + 1)
                dve.tensor_copy(VC[:, :, :], bank(5).rearrange("p (t n) -> p t n", t=NT)).then_inc(dve_evac, 1)
                mixed_low(0, 0, 0)
                mixed_low(1, HD, 0)
                own(8)
                own(9)
                absolute(3)
                for t in range(2, 4):
                    dve.wait_ge(vbp_made, l * 4 + t + 1)
                    dve.tensor_copy(VB[:, t, :], bank(2 + t)).then_inc(dve_evac, 1)
                mixed_low(2, 0, 1)
                softplus(3)
                query_rope(0)
                query_rope(1)
                mixed_low(3, HD, 1)

                def maxima_b(h):
                    for k, t in enumerate(B_ORDER):
                        dve.wait_ge(s_made, l * 32 + 4 * h + max(k, 1) + 1)
                        m = dve.reduce_max(mx[:, h % 2, t:t + 1], b_scores(t), axis=AXX)
                    link(m)
                    ts(nm[:, h % 2, :], mx[:, h % 2, :], -(QK_B ** -0.5), None, ALU.mult).then_inc(nm_made, 1)

                def sums_b(h):
                    dve.wait_ge(p_made, l * 32 + 4 * h + 4)
                    dve.reciprocal(rden[:, h % 2, :], den[:, h % 2, :]).then_inc(rden_made, 1)

                def window_logits(c):
                    dve.wait_ge(sc_made, l * 4 + c + 1)
                    wv = W[c % 2][:, 0:1024].rearrange("p (t k) -> p t k", t=NT)
                    if c >= 2:
                        dve.wait_ge(ptc_made, l * 4 + c - 1)
                    link(stt(W[c % 2][:, 0:1024], DIST[:, :, :].rearrange("p t k -> p (t k)"), -SLOPES[c],
                             PS[:, 1024 * (c % 2):1024 * (c % 2) + 1024], ALU.mult, ALU.add))
                    link(dve.reduce_max(mx[:, c % 2, :], wv, axis=AXX))
                    ts(nm[:, c % 2, :], mx[:, c % 2, :], vec[:, V_SINK + c:V_SINK + c + 1], -1.0, ALU.max, ALU.mult)\
                        .then_inc(nmc_made, 1)

                def sums_c(c):
                    dve.wait_ge(pc_made, l * 20 + 5 * c + 5)
                    link(tt(den[:, c % 2, :], den[:, c % 2, :], esink[:, c % 2, :], ALU.add))
                    dve.reciprocal(rden[:, c % 2, :], den[:, c % 2, :]).then_inc(rden_made, 1)

                maxima_b(0)
                query_rope(2)
                sums_b(0)
                for h in range(NH_B):
                    if h + 1 < NH_B:
                        maxima_b(h + 1)
                    else:
                        window_logits(0)
                    dve.wait_ge(pt_made, l * 8 + h + 1)
                    dve.tensor_copy(W[2][:, 512:896], bank(4, 0, 384)).then_inc(ptd_made, 1)
                    dve.tensor_copy(W[2][:, 1152:1280], bank(4, 384, 512)).then_inc(ptd_made, 1)
                    if h >= 1:
                        mixed_low(3 + h, HD * ((h - 1) % 2), 2 + (h - 1) // 2)
                    if h + 1 < NH_B:
                        sums_b(h + 1)
                    if h + 3 < NH_B:
                        query_rope(h + 3)

                sums_c(0)
                window_logits(1)
                mixed_low(11, HD, 5)
                for c in range(NH_C):
                    dve.wait_ge(ptc_made, l * 4 + c + 1)
                    dve.tensor_copy(W[2][:, 512:896], bank(5, 0, 384)).then_inc(ptd_made, 1)
                    if c + 1 < NH_C:
                        sums_c(c + 1)
                    if c + 2 < NH_C:
                        window_logits(c + 2)
                    if c == 2:
                        low(9, l)
                    mixed_low(12 + c, HD * (c % 2), 6 + c // 2)

                for n in range(P_OUT, P_FF):
                    for t in range(2):
                        o = 2 * (n - P_OUT) + t
                        tile(T_OUT + o + 1)
                        dve.wait_ge(r_init, l * 16 + o + 1)
                        stt(R[:, o, :], bank(OUT_BANK[o]), g1p[:, o:o + 1], R[:, o, :], ALU.mult, ALU.add)\
                            .then_inc(r_made, 1)
                    if n + 1 < P_FF:
                        low(n + 2, l)
                        own(2 * (n - P_OUT) + 10)
                        own(2 * (n - P_OUT) + 11)
                layer_norm_dve(l, 0)

                def quarter(q):
                    for j in range(8):
                        n = P_FF + j
                        for t in range(2):
                            u = 2 * (j % 4) + t
                            if j < 4:
                                dve.wait_ge(relu_made, l * 32 + q * 8 + (u + 1))
                                link(tt(T[2 + u % 2][:, :], T[u % 2][:, :], T[u % 2][:, :], ALU.mult))
                                dve.wait_ge(fh_made, l * 32 + q * 8 + (u + 1))
                                tt(FL[:, u, :], T[2 + u % 2][:, :], FH[:, u, :].bitcast(F32), ALU.subtract)\
                                    .then_inc(fl_made, 1)
                            else:
                                dve.wait_ge(tile_done, l * TILES + q * 16 + (T_FF + 8 + u + 1))
                                if u == 0:
                                    dve.wait_ge(r_init, l * 16 + 16)
                                dve.wait_ge(r_made, l * 40 + q * 8 + 8)
                                stt(R[:, u, :], bank(u % 4), g2p[:, u:u + 1], R[:, u, :], ALU.mult, ALU.add)\
                                    .then_inc(r_made, 1)
                        if isinstance(q, int):
                            if j < 7:
                                low(n + 2, l, q)
                                for i in ((0,), (1, 2), (3,), (4,), (5,), (6,), (7,))[j]:
                                    following(i)
                        else:
                            low(n + 2, l, q)

                n_before = chain.n
                with dve.Fori(0, QUARTERS - 1) as q:
                    chain_base = chain.base
                    chain.base = chain_base + q * links["dve_q"]
                    quarter(q)
                    assert chain.n - n_before == links["dve_q"], ("dve_q", chain.n - n_before)
                chain.base = chain_base
                chain.n = n_before + (QUARTERS - 1) * links["dve_q"]
                quarter(QUARTERS - 1)
                layer_norm_dve(l, 1)
                dve.wait_ge(x_made, l * 16 + 16)
                link(ts(vec[:, :], VEC[:, bass.ds(l + 1, 1), :].rearrange("p a n -> p (a n)"), 1.0, None, ALU.mult))
                assert chain.n == links["dve"], ("dve", chain.n)

        @block.tensor
        def _(pe):
            mm = pe.matmul

            def panel_made(n, l, q=0):
                at = FIRST_ITEMS + (n - 2 if n < 2 else POS[n + 8 * q] if isinstance(q, int)
                                    else POS[P_FF + 1] - 1 + (n - P_FF))
                pe.wait_ge(item_done, l * PER_LAYER + (0 if isinstance(q, int) else q * 8) + (at + 1))

            def product(out, pairs, first=True, last=True):
                for k, (wh, wl, xh, xl) in enumerate(pairs):
                    mm(out, wh, xh, start=first and k == 0, stop=False)
                    mm(out, wh, xl, start=False, stop=False)
                    m = mm(out, wl, xh, start=False, stop=last and k == len(pairs) - 1)
                return m

            def part(n, t, b, k, xh, xl):
                w = lambda W_: W_[:, n % 2, k * 256 + t * P:k * 256 + t * P + P]
                return product(bank(b), [(w(WH), w(WL), xh[:, k, :], xl[:, k, :])], k == 0, k == KT - 1)

            def modulation_sum(b):
                for c in range(ITEM // P):
                    m = mm(bank(b, c, c + 1), acc[:, c * P:(c + 1) * P], CF[:, C_ONE:C_ONE + 1], start=True, stop=True)
                m.then_inc(modsum, 1)

            pe.wait_ge(small_in, 16 * 6)
            pe.wait_ge(item_done, 8)
            modulation_sum(4)

            def layer_norm_pe(l, which):
                ones = CF[:, C_M1024:C_M1024 + P]
                pe.wait_ge(rsum_made, l * 12 + 6 * which + 6)
                mm(bank(6), ones, T[5][:, :], start=True, stop=False)
                pe.wait_ge(r_made, l * 40 + (32 if which else 0) + KT)
                mm(bank(6), ones, R[:, KT - 1, :], start=False, stop=True).then_inc(mean_made, 1)
                last = ("n", KT - 1) if which else ("g", 2 * KT - 1)
                pe.wait_ge(item_done, l * PER_LAYER + (FIRST_ITEMS + POS[last] + 1))
                modulation_sum(4)
                for k in range(2):
                    pe.wait_ge(sqp_made, l * 4 + 2 * which + k + 1)
                    mm(bank(7), ones, T[2 * k][:, :], start=k == 0, stop=False)
                for o in range(4, KT):
                    pe.wait_ge(lsq_made, l * 16 + 8 * which + o + 1)
                    m = mm(bank(7), ones, T[SQUARE_AT[o]][:, :], start=False, stop=o == KT - 1)
                m.then_inc(var_made, 1)

            with pe.Fori(0, DEPTH) as l:
                def evacuated(by_dve=0, by_act=0):
                    if by_dve:
                        pe.wait_ge(dve_evac, l * 10 + by_dve)
                    if by_act:
                        pe.wait_ge(act_evac, l * 4 + by_act)

                def dense(n, t, b):
                    for k in range(KT):
                        m = part(n, t, b, k, HH, HL)
                    m.then_inc(tile_done, 1)

                def dense_tokens(n, lo, width, b, tokens):
                    for i, t in enumerate(tokens):
                        for k in range(KT):
                            cols = slice(k * 256 + lo, k * 256 + lo + width)
                            toks = slice(t * P, t * P + P)
                            out = bank(b, i * width, (i + 1) * width)
                            mm(out, HH[:, k, toks], WH[:, n % 2, cols], start=k == 0, stop=False)
                            mm(out, HL[:, k, toks], WH[:, n % 2, cols], start=False, stop=False)
                            m = mm(out, HH[:, k, toks], WL[:, n % 2, cols], start=False, stop=k == KT - 1)
                    m.then_inc(tile_done, 1)

                panel_made(0, l)
                for k in range(KT):
                    pe.wait_ge(hl_made, l * 16 + k + 1)
                    for t in range(2):
                        m = part(0, t, t, k, HH, HL)
                        if k == KT - 1:
                            m.then_inc(tile_done, 1)
                panel_made(1, l)
                dense(1, 0, 2)
                dense(1, 1, 3)
                pe.wait_ge(sq_made, l * 3 + 2)
                mm(bank(6), CF[:, C_M256:C_M256 + P], T[0][:, :], start=True, stop=False)
                mm(bank(6), CF[:, C_M256:C_M256 + P], T[1][:, :], start=False, stop=True).then_inc(ssq_made, 1)
                panel_made(2, l)
                pe.wait_ge(mods_made, l * 3 + 1)
                dense(2, 0, 4)
                pe.wait_ge(sq_made, l * 3 + 3)
                mm(bank(7), CF[:, C_M128:C_M128 + P], T[2][:, :], start=True, stop=True).then_inc(ssq_made, 1)
                dense(2, 1, 5)
                panel_made(3, l)
                pe.wait_ge(cq_made, l * 2 + 2)
                dense(3, 0, 0)
                dense(3, 1, 1)
                panel_made(4, l)
                pe.wait_ge(krope_made, l * 4 + 4)
                evacuated(by_dve=1)
                dense_tokens(4, 0, 2 * P, 2, (0, 1))
                dense_tokens(4, 0, 2 * P, 3, (2, 3))

                def scores_a(h):
                    rows = slice(HD * (h % 2), HD * (h % 2) + HD)
                    for j in reversed(range(NT)):
                        mm(bank(j, 0, CAUSAL[j]), KA[rows, h // 2, j * P:(j + 1) * P], QA[rows, h // 2, j * P:S],
                           start=True, stop=False)
                        mm(bank(j, 0, P), CB[:, 0:P], CB[:, P:2 * P], start=False, stop=True).then_inc(z_made, 1)

                def suffixes(h):
                    for i in reversed(range(NT)):
                        pe.wait_ge(sp_made, l * 16 + 4 * h + NT - i)
                        for j in range(i, NT):
                            c = C_TRI if j == i else C_NEG1
                            m = mm(bank(i, (j - i) * P, CAUSAL[i]), CF[:, c:c + P],
                                   W[0][:, COFF[j]:COFF[j] + CAUSAL[j]], start=False, stop=True,
                                   skip_group_check=True)
                        m.then_inc(ex_made, 1)

                def values_a(h):
                    pe.wait_ge(w_made, l * 16 + 4 * h + 4)
                    if h >= 2:
                        pe.wait_ge(ol_made, l * 16 + h - 1)
                    row = HD * (h % 2)
                    for j in range(NT):
                        m = mm(PS[row:row + HD, 512 * 6 + j * P:512 * 7],
                               VA[:, j, h * HD:(h + 1) * HD], W[2][:, COFF[j]:COFF[j] + CAUSAL[j]],
                               start=j == 0, stop=j == NT - 1)
                    m.then_inc(o_made, 1)

                def latent_values(t):
                    mm(bank(4 + t % 2), CKVN[:, t * P:(t + 1) * P], UV[:, :], start=True, stop=True).then_inc(vbp_made, 1)

                def key_product(pr):
                    mm(bank(7), UK[:, pr * P:(pr + 1) * P], CKVN[:, :], start=True, stop=True).then_inc(kp_made, 1)

                def query_product(h):
                    w = lambda W_, k: W_[:, P_UQ % 2, k * 1024 + h * P:k * 1024 + h * P + P]
                    product(bank(UQ_BANK[h]), [(w(WH, k), w(WL, k), CQH[:, k, :], CQL[:, k, :]) for k in range(2)])\
                        .then_inc(tile_done, 1)

                def scores_b(h):
                    pe.wait_ge(kn_made, l * 8 + h + 1)
                    pe.wait_ge(qn_made, l * 8 + h + 1)
                    pe.wait_ge(qr_made, l * 8 + h + 1)
                    if h >= 1:
                        pe.wait_ge(p_made, l * 32 + 4 * h)
                    for t in B_ORDER:
                        mm(b_scores(t), QB[0:QK_B, h % 4, t * P:(t + 1) * P], KB[0:QK_B, h % 4, 0:KEYS[t]],
                           start=True, stop=False)
                        mm(b_scores(t)[:, KEYS[t] - CHUNK:KEYS[t]], CB[0:1, 2 * P:3 * P], CB[0:1, 3 * P:3 * P + CHUNK],
                           start=False, stop=True).then_inc(s_made, 1)

                PT_BANK = ((3, 0), (4, 0), (5, 0), (4, 384))
                PT_AT = (0, 512, 896, 1152)

                def transposes_b(h):
                    pe.wait_ge(pn_made, l * 32 + 4 * h + 4)
                    for j in range(NT):
                        b, lo = PT_BANK[j]
                        for t in range(j, NT):
                            m = pe.transpose(bank(b, lo + (t - j) * P, lo + (t - j) * P + P),
                                             W[h % 2][:, KOFF[t] + j * P:KOFF[t] + j * P + P], ident)
                    m.then_inc(pt_made, 1)

                def values_b(h):
                    pe.wait_ge(pta_made, l * 20 + 2 * h + 2)
                    pe.wait_ge(ptd_made, l * 20 + 2 * h + 2)
                    pe.wait_ge(ol_made, l * 16 + 4 + h - 1)
                    row = HD * (h % 2)
                    for j in range(NT):
                        m = mm(PS[row:row + HD, 512 * 6 + j * P:512 * 7], VB[:, j, h * HD:(h + 1) * HD],
                               W[2][:, PT_AT[j]:PT_AT[j] + CAUSAL[j]], start=j == 0, stop=j == NT - 1)
                    m.then_inc(o_made, 1)

                def scores_c(c):
                    if c == 0:
                        pe.wait_ge(p_made, l * 32 + 32)
                    if c >= 2:
                        pe.wait_ge(nmc_made, l * 4 + c - 1)
                    rows = slice(HD * (c // 2), HD * (c // 2) + HD)
                    for t in range(NT):
                        q = QC[rows, c % 2, t * P:(t + 1) * P]
                        at = 1024 * (c % 2) + 256 * t
                        if t == 0:
                            for k in range(2):
                                mm(PS[:, at + k * P:at + k * P + P], q, KC[rows, 0:P], start=True, stop=True)
                        else:
                            m = mm(PS[:, at:at + 2 * P], q, KC[rows, (t - 1) * P:(t + 1) * P], start=True, stop=True)
                    m.then_inc(sc_made, 1)

                def transposes_c(c):
                    wv = W[c % 2][:, 0:1024].rearrange("p (t k) -> p t k", t=NT)
                    pe.wait_ge(pnc_made, l * 16 + 4 * c + 4)
                    for j in range(NT):
                        for k in range(2):
                            if j + k < NT:
                                at = 2048 + 256 * j + k * P
                                m = pe.transpose(PS[:, at:at + P], wv[:, j + k, P * (1 - k):P * (1 - k) + P], ident)
                    m.then_inc(ptc_made, 1)

                def values_c(c):
                    pe.wait_ge(pta_made, l * 20 + 16 + c + 1)
                    pe.wait_ge(ptd_made, l * 20 + 16 + c + 1)
                    pe.wait_ge(ol_made, l * 16 + 12 + c - 1)
                    row = HD * (c % 2)
                    kv = slice(HD * (c // 2), HD * (c // 2) + HD)
                    for t in range(NT):
                        out = PS[row:row + HD, 512 * 6 + t * P:512 * 6 + t * P + P]
                        m = mm(out, VC[:, t, kv], W[2][:, 256 * t:256 * t + P], start=True, stop=t == 0)
                        if t > 0:
                            m = mm(out, VC[:, t - 1, kv], W[2][:, 256 * (t - 1) + P:256 * t], start=False, stop=True)
                    m.then_inc(o_made, 1)

                evacuated(by_dve=5, by_act=2)
                scores_a(0)
                panel_made(5, l)
                dense(5, 0, 4)
                suffixes(0)
                dense(5, 1, 5)
                values_a(0)
                scores_a(1)
                panel_made(6, l)
                evacuated(by_act=3)
                dense(6, 0, 4)
                suffixes(1)
                evacuated(by_act=4)
                dense(6, 1, 5)
                values_a(1)
                scores_a(2)
                pe.wait_ge(item_done, l * PER_LAYER + FIRST_ITEMS + POS["g", 7] + 1)
                modulation_sum(7)
                pe.wait_ge(ukv_in, l * 32 + 32)
                evacuated(by_dve=6)
                latent_values(0)
                evacuated(by_dve=7)
                for t in range(NT):
                    m = pe.transpose(bank(5, t * P, t * P + P), T[3][:, t * P:t * P + P], ident)
                m.then_inc(vc_turned, 1)
                suffixes(2)
                pe.wait_ge(mods_made, l * 3 + 2)
                key_product(0)
                evacuated(by_dve=8)
                latent_values(1)
                values_a(2)
                scores_a(3)
                pe.wait_ge(vb_made, l * 2 + 1)
                latent_values(2)
                pe.wait_ge(vb_made, l * 2 + 2)
                latent_values(3)
                panel_made(P_UQ, l)
                pe.wait_ge(cql_made, l * 2 + 2)
                pe.wait_ge(kn_made, l * 8 + 2)
                query_product(0)
                suffixes(3)
                evacuated(by_dve=9)
                query_product(1)
                values_a(3)

                scores_b(0)
                query_product(2)
                evacuated(by_dve=10)
                for h in range(NH_B):
                    if h + 1 < NH_B:
                        scores_b(h + 1)
                    else:
                        scores_c(0)
                    if h % 2 == 0 and h + 2 < NH_B:
                        pe.wait_ge(qn_made, l * 8 + h + 3)
                        pe.wait_ge(qr_made, l * 8 + h + 3)
                        key_product((h + 2) // 2)
                    if h >= 1:
                        values_b(h - 1)
                    transposes_b(h)
                    if h + 3 < NH_B:
                        if h % 2 == 0:
                            pe.wait_ge(kn_made, l * 8 + h + 4)
                        else:
                            pe.wait_ge(qn_made, l * 8 + h + 3)
                            pe.wait_ge(qr_made, l * 8 + h + 3)
                        query_product(h + 3)
                pe.wait_ge(pta_made, l * 20 + 2 * NH_B)
                scores_c(1)
                values_b(NH_B - 1)

                def out_part(t, k):
                    pe.wait_ge(ol_made, l * 16 + 2 * k + 2)
                    return part(P_OUT, t, OUT_BANK[t], k, HH, HL)

                panel_made(P_OUT, l)
                for k in range(4):
                    out_part(0, k)
                for c in range(NH_C):
                    transposes_c(c)
                    if c + 2 < NH_C:
                        scores_c(c + 2)
                    if c == 2:
                        pe.wait_ge(nmc_made, l * 4 + 3)
                    for t, k in (((0, 4),), ((0, 5),), ((1, 0), (1, 1), (1, 2)), ((1, 3), (1, 4), (1, 5)))[c]:
                        out_part(t, k)
                    values_c(c)
                for n in range(P_OUT, P_FF):
                    panel_made(n, l)
                    for t in range(2):
                        o = 2 * (n - P_OUT) + t
                        if o >= 4:
                            pe.wait_ge(r_made, l * 40 + o - 3)
                        for k in range(6 if o < 2 else 0, KT):
                            m = out_part(o, k) if o < 2 else part(n, t, OUT_BANK[o], k, HH, HL)
                        m.then_inc(tile_done, 1)
                layer_norm_pe(l, 0)

                def quarter(q):
                    for j in range(8):
                        n = P_FF + j
                        panel_made(n, l, q)
                        xh, xl = (HH, HL) if j < 4 else (FH, FL)

                        def bank_free(u):
                            if u < 4:
                                pe.wait_ge(r_made, l * 40 + q * 8 + (8 - 3 + u))
                            elif u < 12:
                                pe.wait_ge(relu_made, l * 32 + q * 8 + (u - 3))
                            else:
                                pe.wait_ge(r_made, l * 40 + q * 8 + (8 + u - 11))

                        if j % 4 == 0:
                            for k in range(KT):
                                pe.wait_ge(*((hl_made, l * 16 + (8 + k + 1)) if j == 0
                                             else (fl_made, l * 32 + q * 8 + (k + 1))))
                                for t in range(2):
                                    if k == 0:
                                        bank_free(2 * j + t)
                                    m = part(n, t, (2 * j + t) % 4, k, xh, xl)
                                    if k == KT - 1:
                                        m.then_inc(tile_done, 1)
                        else:
                            for t in range(2):
                                bank_free(2 * j + t)
                                for k in range(KT):
                                    m = part(n, t, (2 * j + t) % 4, k, xh, xl)
                                m.then_inc(tile_done, 1)

                with pe.Fori(0, QUARTERS - 1) as q:
                    quarter(q)
                quarter(QUARTERS - 1)
                layer_norm_pe(l, 1)


def constants():
    cf = np.zeros((P, NCF), np.float32)
    k = np.arange(P)
    cf[:, C_ID:C_ID + P] = np.eye(P)
    cf[:, C_TRI:C_TRI + P] = -(k[:, None] >= k[None, :]).astype(np.float32)
    cf[:, C_NEG1:C_NEG1 + P] = -1.0
    cf[:, C_M1024:C_M1024 + P] = 1.0 / D
    cf[:, C_M256:C_M256 + P] = 1.0 / Q_LORA
    cf[:, C_M128:C_M128 + P] = 1.0 / KV_LORA
    freq = (np.float32(1.0) / (np.float32(10000.0) ** (np.arange(0, ROPE, 2, dtype=np.float32) / np.float32(ROPE))))
    cf[:, C_FREQ] = freq.astype(np.float32)[k % 16]
    cf[:, C_SIGN] = np.where((k % 32) < 16, -1.0, 1.0)
    cf[:, C_EPS] = LN_EPS
    cf[:, C_ONE] = 1.0
    cf[:, C_ALPHA] = ALPHA
    cb = np.zeros((P, 512), np.float32)
    cb[:, 0:P] = np.eye(P)
    cb[:, P:2 * P] = np.where(k[:, None] >= k[None, :], NEG, 0.0)
    cb[:, 2 * P:3 * P] = np.where(k[None, :] < CHUNK, NEG, 0.0)
    cb[:, 3 * P:] = 1.0
    col = np.arange(2 * P)
    lo = np.where(k < CHUNK, CHUNK, 2 * CHUNK)[:, None]
    maskc = np.where((col[None, :] >= lo) & (col[None, :] < lo + 2 * CHUNK), 0.0, FAR).astype(np.float32)
    return cf, cb, maskc


def panel(w):
    return w.reshape(KT, P, 256).transpose(1, 0, 2).reshape(P, ITEM)


def layer_items(a, l):
    w = a["w_in"][l]
    qa, ka, va, cq, ckv, kr, qc, kc, vc = np.split(w, np.cumsum([256, 256, 256, Q_LORA, KV_LORA, ROPE, 256, 128]), axis=1)
    half = ROPE // 2
    krs = np.concatenate([kr, kr[:, half:], kr[:, :half]], axis=1)
    qc = qc.reshape(D, 2, 2, HD).transpose(0, 2, 1, 3).reshape(D, 256)
    mats = [cq, np.concatenate([ckv, krs, krs], 1), qa, ka, va, qc, np.concatenate([kc, vc], 1)]
    uq = a["w_uq"][l].reshape(Q_LORA, NH_B, QK_B)
    uq = np.concatenate([uq, uq[:, :, NOPE + half:], uq[:, :, NOPE:NOPE + half]], axis=2)
    out = [panel(m) for m in mats]
    out.append(uq.reshape(2, P, 1024).transpose(1, 0, 2).reshape(P, ITEM))
    out += [panel(a["w_out"][l][:, 256 * j:256 * j + 256]) for j in range(4)]
    for q in range(QUARTERS):
        out += [panel(a["w_ff1"][l][:, D * q + 256 * j:D * q + 256 * j + 256]) for j in range(4)]
        out += [panel(a["w_ff2"][l][D * q:D * q + D, 256 * j:256 * j + 256]) for j in range(4)]
    return out


def mod_item(a, l, i):
    third, k = divmod(i, KT)
    return a["ada_w"][l][k * P:(k + 1) * P, third * ITEM:(third + 1) * ITEM]


def column(v):
    return v.reshape(-1, P).T


def layout(a):
    panels = [layer_items(a, l) for l in range(DEPTH)]
    items = [mod_item(a, 0, i) for i in range(8)] + panels[0][:2]
    for l in range(DEPTH):
        nxt = (l + 1) % DEPTH
        for what in ORDER:
            if isinstance(what, tuple):
                items.append(mod_item(a, l, 8 + what[1]) if what[0] == "g" else mod_item(a, nxt, what[1]))
            else:
                items.append(panels[l][what] if what < PANELS else panels[nxt][what - PANELS])
    stream = np.stack(items)
    ukv = []
    vecs = np.zeros((P, DEPTH + 1, NVEC), np.float32)
    for l in range(DEPTH):
        w = a["w_ukv"][l].reshape(KV_LORA, NH_B, NOPE + HD)
        ukv.append(np.concatenate([w[:, :, :NOPE].reshape(P, 512), w[:, :, NOPE:].reshape(P, 512)], axis=1))
    for i in range(DEPTH + 1):
        l = i % DEPTH
        parts = [a[n][l] for n in ("ada_b", "q_norm_g", "kv_norm_g", "ln1_g", "ln1_b", "ln2_g", "ln2_b")]
        vecs[:, i, :V_SINK] = np.concatenate([column(v) for v in parts], axis=1)
        vecs[:, i, V_SINK:V_SINK + NH_C] = np.broadcast_to(a["sinks"][l], (P, NH_C))
    xT = a["x"][0].T.reshape(KT, P, S).transpose(1, 0, 2)
    return {"stream": stream, "ukv": np.stack(ukv), "x": xT, "vecs": vecs, "c": column(a["c"][0]),
            "pos": a["positions"], "posq": a["positions"][0].reshape(NT, P).T}


LINKS = {"act": 8, "dve": 97, "dve_q": 8}


def kernel(**inputs):
    import concourse.bacc as _bacc
    from concourse.bass_utils import run_bass_kernel_spmd as _run

    a = {k: np.asarray(v) for k, v in inputs.items()}
    data = layout(a)
    cf, cb, maskc = constants()
    import ml_dtypes
    data.update(cf=cf, cb=cb.astype(ml_dtypes.bfloat16), maskc=maskc)
    nc = _bacc.Bacc("TRN2", target_bir_lowering=False, num_devices=1)
    arrays, args = {}, []
    for name, v in data.items():
        v = np.ascontiguousarray(v)
        arrays[f"in_{name}"] = v
        args.append(nc.dram_tensor(f"in_{name}", v.shape, mybir.dt.from_np(v.dtype), kind="ExternalInput").ap())
    out = nc.dram_tensor("out_x", (P, KT, S), F32, kind="ExternalOutput").ap()
    build(nc, *args, out, LINKS)
    got = _run(nc, [arrays], core_ids=[0]).results[0]["out_x"]
    return np.ascontiguousarray(np.asarray(got).transpose(1, 0, 2).reshape(D, S).T)[None]
```
